# Optimizing a Trainium2 kernel written in Bass

```python
import jax, jax.numpy as jnp
from jax import lax
import numpy as np
import math

D_MODEL = 1024
BATCH = 1
SEQ = 512
DEPTH = 1

MLA_HEADS = 8
MLA_NOPE = 64
MLA_ROPE = 32
MLA_V = 64
MLA_Q_LORA = 512
MLA_KV_LORA = 256
DIL_HEADS = 8
DIL_HEAD_DIM = 64
DIL_PATTERNS = ((128, 1), (512, 4), (2048, 16))
DIL_WIDTH = DIL_HEADS * DIL_HEAD_DIM
MIX_WIDTH = MLA_HEADS * MLA_V + DIL_WIDTH
IN_COLS = MLA_Q_LORA + MLA_KV_LORA + MLA_ROPE + 3 * DIL_WIDTH
SPLITS = (MLA_Q_LORA,
          MLA_Q_LORA + MLA_KV_LORA,
          MLA_Q_LORA + MLA_KV_LORA + MLA_ROPE,
          MLA_Q_LORA + MLA_KV_LORA + MLA_ROPE + DIL_WIDTH,
          MLA_Q_LORA + MLA_KV_LORA + MLA_ROPE + 2 * DIL_WIDTH)
D_FF = 2816
CONV_WIDTH = 3
ROPE_THETA = 10000.0
EPS = 1e-6
Q_BLOCK = 128
NEG_INF = -1e30


def rms_norm(x, g):
    xf = x.astype(jnp.float32)
    y = xf * lax.rsqrt(jnp.mean(xf * xf, axis=-1, keepdims=True) + EPS)
    return (y * g.astype(jnp.float32)).astype(x.dtype)

def rope(x, positions):
    d = x.shape[-1]
    half = d // 2
    inv_freq = jnp.power(ROPE_THETA, -2.0 * jnp.arange(half, dtype=jnp.float32) / d)
    ang = positions.astype(jnp.float32)[:, :, None, None] * inv_freq
    cos, sin = jnp.cos(ang), jnp.sin(ang)
    xf = x.astype(jnp.float32)
    x1, x2 = xf[..., :half], xf[..., half:]
    return jnp.concatenate([x1 * cos - x2 * sin, x1 * sin + x2 * cos], axis=-1).astype(x.dtype)

def causal_dense_attention(q, k, v, scale):
    B, S, H, Dk = q.shape
    Dv = v.shape[-1]
    nb = S // Q_BLOCK
    qb = q.reshape(B, nb, Q_BLOCK, H, Dk).transpose(1, 0, 2, 3, 4)
    kpos = jnp.arange(S)

    def one_block(args):
        qi, i = args
        s = jnp.einsum('bqhd,bkhd->bhqk', qi, k).astype(jnp.float32) * scale
        qpos = i * Q_BLOCK + jnp.arange(Q_BLOCK)
        mask = kpos[None, :] <= qpos[:, None]
        s = jnp.where(mask, s, NEG_INF)
        p = jax.nn.softmax(s, axis=-1).astype(v.dtype)
        return jnp.einsum('bhqk,bkhd->bqhd', p, v)

    out = lax.map(one_block, (qb, jnp.arange(nb)))
    return out.transpose(1, 0, 2, 3, 4).reshape(B, S, H, Dv)

def banded_causal_attention(q, k, v, span):
    N, L, H, D = q.shape
    blk = span
    nb = -(-L // blk)
    Lp = nb * blk
    pad = ((0, 0), (0, Lp - L), (0, 0), (0, 0))
    q, k, v = jnp.pad(q, pad), jnp.pad(k, pad), jnp.pad(v, pad)
    qb = q.reshape(N, nb, blk, H, D)

    def two_blocks(t):
        tb = jnp.pad(t, ((0, 0), (blk, 0), (0, 0), (0, 0))).reshape(N, nb + 1, blk, H, D)
        return jnp.concatenate([tb[:, :-1], tb[:, 1:]], axis=2)

    kb, vb = two_blocks(k), two_blocks(v)
    s = jnp.einsum('nbqhd,nbkhd->nbhqk', qb, kb).astype(jnp.float32) * (D ** -0.5)
    blk_idx = jnp.arange(nb)[:, None, None]
    qry_pos = blk_idx * blk + jnp.arange(blk)[None, :, None]
    key_pos = (blk_idx - 1) * blk + jnp.arange(2 * blk)[None, None, :]
    dist = qry_pos - key_pos
    mask = (dist >= 0) & (dist <= span) & (key_pos >= 0)
    s = jnp.where(mask[None, :, None], s, NEG_INF)
    m = jnp.max(s, axis=-1, keepdims=True)
    e = jnp.exp(s - m)
    denom = jnp.sum(e, axis=-1, keepdims=True)
    p = (e / denom).astype(v.dtype)
    o = jnp.einsum('nbhqk,nbkhd->nbqhd', p, vb).reshape(N, Lp, H, D)[:, :L]
    lse = (m + jnp.log(denom))[..., 0]
    lse = lse.transpose(0, 1, 3, 2).reshape(N, Lp, H)[:, :L]
    return o, lse

def to_strided(t, dil):
    B, S, H, D = t.shape
    return t.reshape(B, S // dil, dil, H, D).transpose(0, 2, 1, 3, 4).reshape(B * dil, S // dil, H, D)

def dilated_attention(q, k, v):
    B, S, H, D = q.shape
    outs, lses = [], []
    for window, dil in DIL_PATTERNS:
        L = S // dil
        o, lse = banded_causal_attention(to_strided(q, dil), to_strided(k, dil),
                                         to_strided(v, dil), window // dil)
        outs.append(o.reshape(B, dil, L, H, D).transpose(0, 2, 1, 3, 4).reshape(B, S, H, D))
        lses.append(lse.reshape(B, dil, L, H).transpose(0, 2, 1, 3).reshape(B, S, H))
    w = jax.nn.softmax(jnp.stack(lses, axis=0), axis=0)
    out = jnp.sum(w[..., None] * jnp.stack(outs, axis=0).astype(jnp.float32), axis=0)
    return out.astype(q.dtype)

def causal_depthwise_conv(u, w, b):
    K = w.shape[0]
    S = u.shape[1]
    up = jnp.pad(u, ((0, 0), (K - 1, 0), (0, 0)))
    y = b
    for kk in range(K):
        y = y + up[:, kk:kk + S] * w[kk]
    return y

def first_inputs(seed: int = 0) -> dict:
    key = jax.random.key(seed)
    ks = jax.random.split(key, 24)
    nrm = jax.random.normal
    L = DEPTH

    def gain(k, n):
        return 1.0 + 0.05 * nrm(k, (L, n), jnp.float32)

    x = nrm(ks[0], (BATCH, SEQ, D_MODEL), jnp.float32)
    c = nrm(ks[1], (BATCH, D_MODEL), jnp.float32)
    positions = (jnp.arange(SEQ, dtype=jnp.int32)[None, :]
                 + jax.random.randint(ks[2], (BATCH, 1), 0, 4096, dtype=jnp.int32))
    return {
        "x": x,
        "c": c,
        "positions": positions,
        "w_ada": nrm(ks[3], (L, D_MODEL, 6 * D_MODEL), jnp.float32) * (0.5 * D_MODEL ** -0.5),
        "b_ada": 0.02 * nrm(ks[4], (L, 6 * D_MODEL), jnp.float32),
        "g_mix_norm": gain(ks[5], D_MODEL),
        "w_in": nrm(ks[6], (L, D_MODEL, IN_COLS), jnp.float32) * D_MODEL ** -0.5,
        "g_q_lat": gain(ks[7], MLA_Q_LORA),
        "w_q_b": nrm(ks[8], (L, MLA_Q_LORA, MLA_HEADS * (MLA_NOPE + MLA_ROPE)), jnp.float32) * MLA_Q_LORA ** -0.5,
        "g_kv_lat": gain(ks[9], MLA_KV_LORA),
        "w_kv_b": nrm(ks[10], (L, MLA_KV_LORA, MLA_HEADS * (MLA_NOPE + MLA_V)), jnp.float32) * MLA_KV_LORA ** -0.5,
        "g_mla_q_nope": gain(ks[11], MLA_NOPE),
        "g_mla_q_pe": gain(ks[12], MLA_ROPE),
        "g_mla_k_nope": gain(ks[13], MLA_NOPE),
        "g_mla_k_pe": gain(ks[14], MLA_ROPE),
        "g_dil_q": gain(ks[15], DIL_HEAD_DIM),
        "g_dil_k": gain(ks[16], DIL_HEAD_DIM),
        "w_o": nrm(ks[17], (L, MIX_WIDTH, D_MODEL), jnp.float32) * MIX_WIDTH ** -0.5,
        "g_ffn_norm": gain(ks[18], D_MODEL),
        "w_up": nrm(ks[19], (L, D_MODEL, 2 * D_FF), jnp.float32) * D_MODEL ** -0.5,
        "w_conv": nrm(ks[20], (L, CONV_WIDTH, 2 * D_FF), jnp.float32) * CONV_WIDTH ** -0.5,
        "b_conv": 0.02 * nrm(ks[21], (L, 2 * D_FF), jnp.float32),
        "w_down": nrm(ks[22], (L, D_FF, D_MODEL), jnp.float32) * D_FF ** -0.5,
    }

def first_block(x, c, positions, w_ada, b_ada, g_mix_norm, w_in, g_q_lat, w_q_b, g_kv_lat, w_kv_b,
              g_mla_q_nope, g_mla_q_pe, g_mla_k_nope, g_mla_k_pe, g_dil_q, g_dil_k, w_o,
              g_ffn_norm, w_up, w_conv, b_conv, w_down):
    B, S, _ = x.shape
    for l in range(DEPTH):
        mod = jax.nn.silu(c) @ w_ada[l] + b_ada[l]
        sh1, sc1, g1, sh2, sc2, g2 = jnp.split(mod, 6, axis=-1)

        h = rms_norm(x, g_mix_norm[l]) * (1.0 + sc1[:, None]) + sh1[:, None]
        proj = h @ w_in[l]
        q_lat, kv_lat, k_pe, qd, kd, vd = jnp.split(proj, SPLITS, axis=-1)

        q = (rms_norm(q_lat, g_q_lat[l]) @ w_q_b[l]).reshape(B, S, MLA_HEADS, MLA_NOPE + MLA_ROPE)
        q_nope = rms_norm(q[..., :MLA_NOPE], g_mla_q_nope[l])
        q_pe = rope(rms_norm(q[..., MLA_NOPE:], g_mla_q_pe[l]), positions)
        kv = (rms_norm(kv_lat, g_kv_lat[l]) @ w_kv_b[l]).reshape(B, S, MLA_HEADS, MLA_NOPE + MLA_V)
        k_nope = rms_norm(kv[..., :MLA_NOPE], g_mla_k_nope[l])
        v_mla = kv[..., MLA_NOPE:]
        k_pe = rope(rms_norm(k_pe, g_mla_k_pe[l])[:, :, None, :], positions)
        k_mla = jnp.concatenate([k_nope, jnp.broadcast_to(k_pe, (B, S, MLA_HEADS, MLA_ROPE))], axis=-1)
        q_mla = jnp.concatenate([q_nope, q_pe], axis=-1)
        o_mla = causal_dense_attention(q_mla, k_mla, v_mla, (MLA_NOPE + MLA_ROPE) ** -0.5)

        qd = rope(rms_norm(qd.reshape(B, S, DIL_HEADS, DIL_HEAD_DIM), g_dil_q[l]), positions)
        kd = rope(rms_norm(kd.reshape(B, S, DIL_HEADS, DIL_HEAD_DIM), g_dil_k[l]), positions)
        vd = vd.reshape(B, S, DIL_HEADS, DIL_HEAD_DIM)
        o_dil = dilated_attention(qd, kd, vd)

        mix = jnp.concatenate([o_mla.reshape(B, S, MLA_HEADS * MLA_V),
                               o_dil.reshape(B, S, DIL_WIDTH)], axis=-1) @ w_o[l]
        x = x + g1[:, None] * mix

        h2 = rms_norm(x, g_ffn_norm[l]) * (1.0 + sc2[:, None]) + sh2[:, None]
        u = causal_depthwise_conv(h2 @ w_up[l], w_conv[l], b_conv[l])
        gate, val = jnp.split(u, 2, axis=-1)
        x = x + g2[:, None] * ((jax.nn.silu(gate) * val) @ w_down[l])
    return x


N_META = 16
SSM_WIDTH = 1024
SSM_GROUP = 16
SSM_GROUPS = SSM_WIDTH // SSM_GROUP
SSM_STATE = 64
DT_MIN = 1e-3
DT_MAX = 1e-1
HGRN_WIDTH = 1024
HGRN_HEAD_DIM = 128
HGRN_HEADS = HGRN_WIDTH // HGRN_HEAD_DIM
HGRN_CHUNK = 16
IN_COLS_2 = SSM_WIDTH + 4 * HGRN_WIDTH + 2 * D_MODEL


def rmsnorm(x, g):
    xf = x.astype(jnp.float32)
    y = xf * lax.rsqrt(jnp.mean(xf * xf, axis=-1, keepdims=True) + EPS)
    return (y * g.astype(jnp.float32)).astype(x.dtype)

def _complex_affine_combine(e1, e2):
    a1r, a1i, b1r, b1i = e1
    a2r, a2i, b2r, b2i = e2
    ar = a1r * a2r - a1i * a2i
    ai = a1r * a2i + a1i * a2r
    br = a2r * b1r - a2i * b1i + b2r
    bi = a2r * b1i + a2i * b1r + b2i
    return ar, ai, br, bi

def s5_mixer(u, lam_re, lam_im, log_dt, b_re, b_im, c_re, c_im, d_skip, w_glu):
    bsz, L, _ = u.shape
    uf = u.astype(jnp.float32).reshape(bsz, L, SSM_GROUPS, SSM_GROUP)
    lr = lam_re.astype(jnp.float32)
    li = lam_im.astype(jnp.float32)
    dt = jnp.exp(log_dt.astype(jnp.float32))[:, None]
    mag = jnp.exp(lr * dt)
    ab_re = mag * jnp.cos(li * dt)
    ab_im = mag * jnp.sin(li * dt)
    den = lr * lr + li * li
    nr = ab_re - 1.0
    coef_re = (nr * lr + ab_im * li) / den
    coef_im = (ab_im * lr - nr * li) / den
    br = b_re.astype(jnp.float32)
    bi = b_im.astype(jnp.float32)
    bb_re = coef_re[..., None] * br - coef_im[..., None] * bi
    bb_im = coef_re[..., None] * bi + coef_im[..., None] * br
    v_re = jnp.einsum('blgh,gph->blgp', uf, bb_re)
    v_im = jnp.einsum('blgh,gph->blgp', uf, bb_im)
    a_re = jnp.broadcast_to(ab_re[None, None], (1, L, SSM_GROUPS, SSM_STATE))
    a_im = jnp.broadcast_to(ab_im[None, None], (1, L, SSM_GROUPS, SSM_STATE))
    _, _, s_re, s_im = lax.associative_scan(_complex_affine_combine, (a_re, a_im, v_re, v_im), axis=1)
    y = (jnp.einsum('blgp,ghp->blgh', s_re, c_re.astype(jnp.float32))
         - jnp.einsum('blgp,ghp->blgh', s_im, c_im.astype(jnp.float32))
         + d_skip.astype(jnp.float32).reshape(SSM_GROUPS, SSM_GROUP) * uf)
    y = jax.nn.gelu(y.reshape(bsz, L, SSM_WIDTH)).astype(u.dtype)
    return y * jax.nn.sigmoid(y @ w_glu)

def hgrn2_mixer(q, f_logit, i_in, og, lb, norm_g):
    bsz, L, _ = q.shape
    n_chunks = L // HGRN_CHUNK

    def heads(t):
        return t.reshape(bsz, n_chunks, HGRN_CHUNK, HGRN_HEADS, HGRN_HEAD_DIM).transpose(1, 0, 3, 2, 4)

    lbf = lb.astype(jnp.float32)
    f = lbf + (1.0 - lbf) * jax.nn.sigmoid(f_logit.astype(jnp.float32))
    log_f = jnp.log(f)
    qh = heads(q.astype(jnp.float32))
    kh = heads(1.0 - f)
    vh = heads(i_in.astype(jnp.float32))
    cum = jnp.cumsum(heads(log_f), axis=3)
    q_in = qh * jnp.exp(cum)
    k_in = kh * jnp.exp(-cum)
    k_out = kh * jnp.exp(cum[..., -1:, :] - cum)
    chunk_decay = jnp.exp(cum[..., -1, :])
    causal = jnp.tril(jnp.ones((HGRN_CHUNK, HGRN_CHUNK), dtype=bool))

    def chunk_step(state, xs):
        qi, ki, ko, v, dec = xs
        scores = jnp.where(causal, jnp.einsum('bhtd,bhsd->bhts', qi, ki), 0.0)
        o = jnp.einsum('bhts,bhsv->bhtv', scores, v) + jnp.einsum('bhtd,bhdv->bhtv', qi, state)
        state = dec[..., None] * state + jnp.einsum('bhsd,bhsv->bhdv', ko, v)
        return state, o

    init = jnp.zeros((bsz, HGRN_HEADS, HGRN_HEAD_DIM, HGRN_HEAD_DIM), jnp.float32)
    _, o = lax.scan(chunk_step, init, (q_in, k_in, k_out, vh, chunk_decay))
    o = o.transpose(1, 0, 3, 2, 4).reshape(bsz, L, HGRN_HEADS, HGRN_HEAD_DIM)
    o = o * lax.rsqrt(jnp.mean(o * o, axis=-1, keepdims=True) + EPS) * norm_g.astype(jnp.float32)
    o = o.reshape(bsz, L, HGRN_WIDTH).astype(q.dtype)
    return o * jax.nn.silu(og)

def causal_dwconv(u, w, b):
    L = u.shape[1]
    up = jnp.pad(u, ((0, 0), (CONV_WIDTH - 1, 0), (0, 0)))
    out = b
    for j in range(CONV_WIDTH):
        out = out + up[:, j:j + L, :] * w[j]
    return out

def second_inputs(seed: int = 0) -> dict:
    key = jax.random.key(seed)
    ks = jax.random.split(key, 24)
    f32 = jnp.float32

    def nrm(k, shape, scale):
        return jax.random.normal(k, shape, f32) * scale

    n_idx = jnp.arange(SSM_STATE, dtype=f32)
    return {
        'x': nrm(ks[0], (BATCH, SEQ, D_MODEL), 1.0),
        'meta_tokens': nrm(ks[1], (N_META, D_MODEL), 1.0),
        'mix_norm_g': 1.0 + nrm(ks[2], (DEPTH, D_MODEL), 0.02),
        'w_in': nrm(ks[3], (DEPTH, D_MODEL, IN_COLS_2), D_MODEL ** -0.5),
        'ssm_lambda_re': -0.5 + nrm(ks[4], (DEPTH, SSM_GROUPS, SSM_STATE), 0.01),
        'ssm_lambda_im': math.pi * n_idx + nrm(ks[5], (DEPTH, SSM_GROUPS, SSM_STATE), 0.01),
        'ssm_log_dt': jax.random.uniform(ks[6], (DEPTH, SSM_GROUPS), f32, math.log(DT_MIN), math.log(DT_MAX)),
        'ssm_b_re': nrm(ks[7], (DEPTH, SSM_GROUPS, SSM_STATE, SSM_GROUP), (2 * SSM_GROUP) ** -0.5),
        'ssm_b_im': nrm(ks[8], (DEPTH, SSM_GROUPS, SSM_STATE, SSM_GROUP), (2 * SSM_GROUP) ** -0.5),
        'ssm_c_re': nrm(ks[9], (DEPTH, SSM_GROUPS, SSM_GROUP, SSM_STATE), SSM_STATE ** -0.5),
        'ssm_c_im': nrm(ks[10], (DEPTH, SSM_GROUPS, SSM_GROUP, SSM_STATE), SSM_STATE ** -0.5),
        'ssm_d': nrm(ks[11], (DEPTH, SSM_WIDTH), 1.0),
        'ssm_w_glu': nrm(ks[12], (DEPTH, SSM_WIDTH, SSM_WIDTH), SSM_WIDTH ** -0.5),
        'w_ssm_proj': nrm(ks[13], (DEPTH, SSM_WIDTH, D_MODEL), SSM_WIDTH ** -0.5),
        'hgrn_lb_logits': nrm(ks[14], (DEPTH + 1, HGRN_WIDTH), 0.1),
        'hgrn_norm_g': 1.0 + nrm(ks[15], (DEPTH, HGRN_HEAD_DIM), 0.02),
        'w_hgrn_proj': nrm(ks[16], (DEPTH, HGRN_WIDTH, D_MODEL), HGRN_WIDTH ** -0.5),
        'w_out': nrm(ks[17], (DEPTH, D_MODEL, D_MODEL), D_MODEL ** -0.5),
        'ffn_norm_g': 1.0 + nrm(ks[18], (DEPTH, D_MODEL), 0.02),
        'w_up': nrm(ks[19], (DEPTH, D_MODEL, 2 * D_FF), D_MODEL ** -0.5),
        'conv_w': nrm(ks[20], (DEPTH, CONV_WIDTH, 2 * D_FF), CONV_WIDTH ** -0.5),
        'conv_b': nrm(ks[21], (DEPTH, 2 * D_FF), 0.01),
        'w_down': nrm(ks[22], (DEPTH, D_FF, D_MODEL), D_FF ** -0.5),
        'final_norm_g': 1.0 + nrm(ks[23], (D_MODEL,), 0.02),
    }

def second_block(x, meta_tokens, mix_norm_g, w_in, ssm_lambda_re, ssm_lambda_im, ssm_log_dt,
              ssm_b_re, ssm_b_im, ssm_c_re, ssm_c_im, ssm_d, ssm_w_glu, w_ssm_proj,
              hgrn_lb_logits, hgrn_norm_g, w_hgrn_proj, w_out, ffn_norm_g, w_up, conv_w,
              conv_b, w_down, final_norm_g):
    bsz = x.shape[0]
    meta = jnp.broadcast_to(meta_tokens.astype(x.dtype)[None], (bsz, N_META, D_MODEL))
    h = jnp.concatenate([meta, x], axis=1)
    lower_bounds = jnp.cumsum(jax.nn.softmax(hgrn_lb_logits.astype(jnp.float32), axis=0), axis=0)
    o1 = SSM_WIDTH
    o2 = o1 + HGRN_WIDTH
    o3 = o2 + HGRN_WIDTH
    o4 = o3 + HGRN_WIDTH
    o5 = o4 + HGRN_WIDTH
    o6 = o5 + D_MODEL
    for l in range(DEPTH):
        z = rmsnorm(h, mix_norm_g[l])
        p = z @ w_in[l]
        y_a = s5_mixer(p[..., :o1], ssm_lambda_re[l], ssm_lambda_im[l], ssm_log_dt[l],
                       ssm_b_re[l], ssm_b_im[l], ssm_c_re[l], ssm_c_im[l], ssm_d[l], ssm_w_glu[l])
        y_b = hgrn2_mixer(p[..., o1:o2], p[..., o2:o3], p[..., o3:o4], p[..., o4:o5],
                          lower_bounds[l], hgrn_norm_g[l])
        merged = (jax.nn.sigmoid(p[..., o5:o6]) * (y_a @ w_ssm_proj[l])
                  + jax.nn.sigmoid(p[..., o6:]) * (y_b @ w_hgrn_proj[l]))
        h = h + merged @ w_out[l]
        z = rmsnorm(h, ffn_norm_g[l])
        u = causal_dwconv(z @ w_up[l], conv_w[l], conv_b[l])
        h = h + (jax.nn.silu(u[..., :D_FF]) * u[..., D_FF:]) @ w_down[l]
    return rmsnorm(h[:, N_META:], final_norm_g)


def setup_inputs(seed=0):
    out = dict(first_inputs(seed))
    for name, value in second_inputs(seed + 1).items():
        if name != "x":
            out[name + "_2"] = value
    return out


def reference(
    x, c, positions, w_ada, b_ada, g_mix_norm, w_in, g_q_lat, w_q_b, g_kv_lat, w_kv_b,
    g_mla_q_nope, g_mla_q_pe, g_mla_k_nope, g_mla_k_pe, g_dil_q, g_dil_k, w_o, g_ffn_norm, w_up,
    w_conv, b_conv, w_down, meta_tokens_2, mix_norm_g_2, w_in_2, ssm_lambda_re_2,
    ssm_lambda_im_2, ssm_log_dt_2, ssm_b_re_2, ssm_b_im_2, ssm_c_re_2, ssm_c_im_2, ssm_d_2,
    ssm_w_glu_2, w_ssm_proj_2, hgrn_lb_logits_2, hgrn_norm_g_2, w_hgrn_proj_2, w_out_2,
    ffn_norm_g_2, w_up_2, conv_w_2, conv_b_2, w_down_2, final_norm_g_2,
):
    x = first_block(
        x, c, positions, w_ada, b_ada, g_mix_norm, w_in, g_q_lat, w_q_b, g_kv_lat, w_kv_b,
        g_mla_q_nope, g_mla_q_pe, g_mla_k_nope, g_mla_k_pe, g_dil_q, g_dil_k, w_o, g_ffn_norm,
        w_up, w_conv, b_conv, w_down,
    )
    return second_block(
        x, meta_tokens_2, mix_norm_g_2, w_in_2, ssm_lambda_re_2, ssm_lambda_im_2, ssm_log_dt_2,
        ssm_b_re_2, ssm_b_im_2, ssm_c_re_2, ssm_c_im_2, ssm_d_2, ssm_w_glu_2, w_ssm_proj_2,
        hgrn_lb_logits_2, hgrn_norm_g_2, w_hgrn_proj_2, w_out_2, ffn_norm_g_2, w_up_2, conv_w_2,
        conv_b_2, w_down_2, final_norm_g_2,
    )


_drawn_inputs = setup_inputs


def setup_inputs(seed=0):
    import zlib

    import numpy as np

    out = dict(_drawn_inputs(seed))
    spreads = {}
    factors = {'g_mix_norm': 8.0,
     'g_q_lat': 8.0,
     'g_kv_lat': 8.0,
     'g_mla_q_nope': 8.0,
     'g_mla_q_pe': 8.0,
     'g_mla_k_nope': 8.0,
     'g_mla_k_pe': 8.0,
     'g_dil_q': 8.0,
     'g_dil_k': 8.0,
     'g_ffn_norm': 2.914,
     'b_conv': 7.138,
     'mix_norm_g_2': 3.794,
     'ssm_lambda_re_2': 64.0,
     'ssm_lambda_im_2': 26.2,
     'ssm_log_dt_2': 27.784,
     'ssm_b_re_2': 36.216,
     'ssm_b_im_2': 36.768,
     'ssm_c_re_2': 37.024,
     'ssm_c_im_2': 36.824,
     'hgrn_norm_g_2': 26.353,
     'ffn_norm_g_2': 12.32,
     'conv_b_2': 25.539,
     'final_norm_g_2': 8.117}
    for name, (base, spread) in spreads.items():
        noise = np.random.default_rng([zlib.crc32(name.encode()), seed]).standard_normal(out[name].shape)
        drawn = base * np.exp(spread * noise) if base else spread * noise
        out[name] = __import__('jax').numpy.asarray(drawn.astype(out[name].dtype))
    for name, factor in factors.items():
        out[name] = (out[name] * factor).astype(out[name].dtype)
    return out
```

```python
from contextlib import ExitStack

import numpy as np

import concourse.bass as bass
from concourse import mybir

ALU = mybir.AluOpType
ACT = mybir.ActivationFunctionType
F32 = mybir.dt.float32
F32R = mybir.dt.float32r
I32 = mybir.dt.int32

P = 128
D = 1024
KD = D // P
META = 16
SEQ = 512
T1, T2 = SEQ, META + SEQ
HT2 = T2 // 2
QB = SEQ // P
TB2 = -(-T2 // P)
LC = 8
NC5 = T2 // LC
SG, SH, SP = 64, 16, 64
PAIRS = SG // 2
BP, NB5 = 4, 8
CK = 16
NCK = T2 // CK
NB32 = NCK // 2
HEADS = 8
HD = 64
RD = 32
QL, KVL = 512, 256
FF = 2816
NF = FF // P
EPS = 1e-6
NEG = -1e30
UNIT = 1024
NST, NHL = 2, 4
PRE = 4
LEAD = 3
NLN = 4

PARAMS = [("b_ada", "b_ada", 48), ("c", "c", 8), ("g_mix", "g_mix_norm", 8), ("g_ql", "g_q_lat", 4),
          ("g_kvl", "g_kv_lat", 2), ("g_ffn", "g_ffn_norm", 8), ("cb", "b_conv", 44), ("cw", "w_conv", 132),
          ("g_mix2", "mix_norm_g_2", 8), ("g_ffn2", "ffn_norm_g_2", 8), ("g_fin", "final_norm_g_2", 8),
          ("ssm_d", "ssm_d_2", 8), ("lb", "hgrn_lb_logits_2", 16), ("hg", "hgrn_norm_g_2", 1),
          ("cb2", "conv_b_2", 44), ("cw2", "conv_w_2", 132)]
HEAD_PARAMS = [("gdq", "g_dil_q", 2), ("gdk", "g_dil_k", 2), ("gqn", "g_mla_q_nope", 2), ("gkn", "g_mla_k_nope", 2),
               ("gqp", "g_mla_q_pe", 4), ("gkp", "g_mla_k_pe", 4)]
ROW, NROWS = {}, 0
for _n, _, _k in PARAMS:
    ROW[_n], NROWS = NROWS, NROWS + _k
for _n, _, _ in HEAD_PARAMS:
    ROW[_n], NROWS = NROWS, NROWS + 1
NBLK = -(-NROWS // P)


def host_constants():
    p = np.arange(P)
    ident = np.eye(P)
    ones = np.ones((P, P))
    b64 = (p[:, None] // 64 == p[None] // 64) * 1.0
    b32 = (p[:, None] // 32 == p[None] // 32) * 1.0

    def rot(w):
        r = np.zeros((P, P))
        for m in range(P):
            j = m % w
            if j < w // 2:
                r[m + w // 2, m] = -1.0
            else:
                r[m - w // 2, m] = 1.0
        return r

    qi, ki = p[:, None], p[None]
    tri = np.where(ki <= qi, 0.0, NEG)

    def count(delta):
        d = P * delta + qi - ki
        c = (((d >= 0) & (d <= 128)) * 1 + ((d >= 0) & (d % 4 == 0)) * 1 + ((d >= 0) & (d % 16 == 0)) * 1)
        return np.where(c > 0, np.log(np.maximum(c, 1)) / HD ** -0.5, NEG)

    mla = [np.zeros((P, P))] * 3 + [tri]
    dil = [count(3), count(2), count(1), count(0)]
    inv64 = (10000.0 ** (-2.0 * (p % 32) / 64)).astype(np.float32)
    inv32 = (10000.0 ** (-2.0 * (p % 16) / 32)).astype(np.float32)
    chunk = ((p[:, None] // 16 == p[None] // 16) & (p[:, None] <= p[None])) * 1.0
    misc = np.zeros((P, P))
    misc[:, 0], misc[:, 1] = inv64, inv32
    misc[:, 64:] = p[:, None] // 16 == 2 * (p[None, :64] // 16)
    return np.concatenate([ident, ones, b64, b32, rot(64), rot(32)] + mla + dil + [chunk, misc],
                          axis=1).astype(np.float32)


CONST = {n: i * P for i, n in enumerate(["ident", "ones", "b64", "b32", "r64", "r32", "mla", "_m1", "_m2", "_m3",
                                         "dil", "_d1", "_d2", "_d3", "chunk", "misc"])}
NCONST = len(CONST) * P

PI = float(np.float32(np.pi))
TWO_PI_HI = 6.28125
TWO_PI_LO = 2 * np.pi - TWO_PI_HI
MAGIC = 1.5 * 2.0 ** 23

INPUTS = ["x", "c", "positions", "w_ada", "b_ada", "g_mix_norm", "w_in", "g_q_lat", "w_q_b", "g_kv_lat", "w_kv_b",
          "g_mla_q_nope", "g_mla_q_pe", "g_mla_k_nope", "g_mla_k_pe", "g_dil_q", "g_dil_k", "w_o", "g_ffn_norm",
          "w_up", "w_conv", "b_conv", "w_down", "meta_tokens_2", "mix_norm_g_2", "w_in_2", "ssm_lambda_re_2",
          "ssm_lambda_im_2", "ssm_log_dt_2", "ssm_b_re_2", "ssm_b_im_2", "ssm_c_re_2", "ssm_c_im_2", "ssm_d_2",
          "ssm_w_glu_2", "w_ssm_proj_2", "hgrn_lb_logits_2", "hgrn_norm_g_2", "w_hgrn_proj_2", "w_out_2",
          "ffn_norm_g_2", "w_up_2", "conv_w_2", "conv_b_2", "w_down_2", "final_norm_g_2"]


class Plan:

    def __init__(self):
        self.load_of, self.free, self.full = [], [], []
        self.unit0, self.job0 = {}, {}
        self.loads = []
        self.mark = 0
        self.n_ada = 0

    def gemm(self, name, n, dmas=1):
        self.unit0[name], self.job0[name] = len(self.free), len(self.full)
        for i in range(n):
            self.mark += 1
            self.loads.append(("w", len(self.free), dmas[i] if isinstance(dmas, list) else dmas))
            self.free.append(self.mark)
            self.full.append(self.mark)

    def shared(self, name, units, jobs, dmas=1):
        self.unit0[name], self.job0[name] = len(self.free), len(self.full)
        self.full += [self.mark + 1 + j for j in range(jobs)]
        self.mark += jobs
        for i in range(units):
            self.loads.append(("w", len(self.free), dmas[i] if isinstance(dmas, list) else dmas))
            self.free.append(self.mark)

    def ada(self, n):
        for _ in range(n):
            self.loads.append(("ada", self.n_ada, 1))
            self.n_ada += 1

    def close(self):
        sums = [0] * NST
        self.landed = []
        self.ada_load, self.w_load = [], []
        for n, (kind, i, d) in enumerate(self.loads):
            sums[n % NST] += 16 * d
            self.landed.append((n % NST, sums[n % NST]))
            (self.ada_load if kind == "ada" else self.w_load).append(n)


def make_plan():
    p = Plan()
    p.ada(16 - PRE)
    p.gemm("ql", 4)
    p.gemm("kvl", 2)
    p.gemm("kpe", 1, 4)
    p.gemm("dq", 4)
    p.gemm("dk", 4)
    p.shared("dv", 4, QB)
    p.shared("qn01", 1, 2, 8)
    p.shared("qn23", 1, 2, 8)
    p.shared("qp", 1, 2, 8)
    p.shared("kn", 1, 4, 8)
    p.shared("mv", 1, QB, 2)
    p.ada(32)
    p.gemm("wo", 8)
    for c in FFN_ORDER:
        p.gemm("b1" + c[0] + str(c[1]), c[2])
    p.gemm("u", 8)
    p.gemm("q", 8)
    p.gemm("glu", 8)
    p.gemm("f", 8)
    p.shared("i0", 4, TB2)
    p.shared("i1", 4, TB2)
    p.gemm("og", 8)
    p.gemm("mrg", 32)
    p.gemm("out", 8)
    for c in FFN_ORDER:
        p.gemm("b2" + c[0] + str(c[1]), c[2])
    return p


CH = [8, 8, 6]
FFN_ORDER = [("up", 0, 16), ("up", 1, 16), ("down", 0, 8), ("up", 2, 12), ("down", 1, 8), ("down", 2, 8)]


def emit(nc, A, out):
    plan = make_plan()
    plan.close()
    ctx = ExitStack()
    with ctx:
        def sem(name):
            return ctx.enter_context(nc.semaphore(name))

        base = -(-nc.sbuf_base // 64) * 64
        end = nc.sbuf_usable_end

        def at(name, shape, off, dt=F32):
            n = 4 * int(np.prod(shape[1:]))
            assert base + off + n <= end, (name, base + off + n - end)
            return nc.alloc_sbuf_tensor_at(name, shape, dt, offset=base + off)

        cst = at("cst", [P, NCONST], 0)
        o = 4 * NCONST
        par = at("par", [P, 512], o)
        mod = at("mod", [P, 48], o + 2048)
        gsc = at("gsc", [P, 4, 8], o + 2240)
        csil = at("csil", [P, 8], o + 2368)
        small = at("small", [P, 64], o + 2400)
        o += 3072
        stage = [at(f"stage{i}", [P, UNIT], o + 4096 * i) for i in range(NST)]
        o += 4096 * NST
        whi = [at(f"whi{i}", [P, UNIT], o + 4096 * i, F32R) for i in range(NHL)]
        o += 4096 * NHL
        wlo = [at(f"wlo{i}", [P, UNIT], o + 4096 * i, F32R) for i in range(NHL)]
        o += 4096 * NHL
        xT = at("xT", [P, KD, T2], o)
        o += 4 * KD * T2
        NZU = 3
        ZUO = o
        zu = at("zu", [P, NZU, T2], o)
        o += 4 * NZU * T2
        SQO = o
        sq = at("sq", [P, 2, T2], o)
        o += 8 * T2
        RSO = o
        rs = at("rs", [P, T2], o)
        o += 4 * T2
        ZREG = o
        zhi = at("zhi", [P, KD, T2], o, F32R)
        zlo = at("zlo", [P, KD, T2], o + 4 * KD * T2, F32R)
        sqg = [at(f"sqg{i}", [P, NLN, T1], ZREG + 8192 * i) for i in range(2)]
        rt = [at(f"rt{i}", [P, NLN, T1], ZREG + 16384 + 8192 * i) for i in range(2)]
        mhi = at("mhi", [P, KD, T1], ZREG, F32R)
        mlo = at("mlo", [P, KD, T1], ZREG + 16384, F32R)
        o += 8 * KD * T2
        FREE = o
        HT = at("HT", [P, 19, T1], FREE)
        xrow = at("xrow", [P, QB, D], FREE)
        early = [at(f"early{i}", [P, UNIT], FREE + 16384 + 4096 * i) for i in range(PRE)]
        Vm = at("Vm", [P, QB, 512], FREE + 38912)
        Vd = at("Vd", [P, QB, 512], FREE + 38912 + 8192)
        prow = at("prow", [P, NBLK, P], FREE + 38912)
        posi = at("posi", [P, T1], FREE + 38912 + 2048, I32)
        metar = at("metar", [META, D], FREE + 38912 + 8192)
        LAT = FREE + 38912 + 16384
        lhi = at("lhi", [P, 6, T1], LAT, F32R)
        llo = at("llo", [P, 6, T1], LAT + 12288, F32R)
        pb = at("pb", [P, 4, T1], LAT)
        PT = at("PT", [P, 3, T1], LAT + 8192)
        posf = at("posf", [P, T1], FREE + 38912 + 4096)
        angt = at("angt", [P, 2, T1], FREE + 38912 + 8192 + 4096)
        TAB = LAT + 24576
        asum = [at(f"asum{i}", [P, D], LAT + 14336 + 4096 * i) for i in range(2)]
        tab = at("tab", [P, 4, T1], TAB)
        ghi = [at(f"ghi{i}", [P, 8, T2], FREE + 16896 * i, F32R) for i in range(2)]
        glo = [at(f"glo{i}", [P, 8, T2], FREE + 33792 + 16896 * i, F32R) for i in range(2)]
        ub = at("ub", [P, 2, 2 + T2], FREE + 67584)
        cv = at("cv", [P, 2, 2, T2], FREE + 67584 + 4256)

        R8 = 4 * KD * T2
        uD = at("uD", [P, KD, LC, NC5], FREE)
        Y5 = at("Y5", [P, SG, NC5], FREE + R8)
        U5 = at("U5", [P, SG, NC5], FREE + R8)
        yT = at("yT", [P, KD, LC, NC5], FREE + 2 * R8)
        S5 = at("S5", [P, PAIRS, 2, NC5 + 1], FREE + 2 * R8)
        y5 = at("y5", [P, KD, T2], FREE + R8)
        W5 = FREE + 2 * R8 + 4 * PAIRS * 2 * (NC5 + 1)
        W5 = -(-W5 // 64) * 64
        _w = [W5]

        def w5(name, shape, dt=F32):
            off = _w[0]
            _w[0] += -(-4 * int(np.prod(shape[1:])) // 32) * 32
            return at(name, shape, off, dt), off

        s5row, _ = w5("s5row", [PAIRS, 3, P])
        crow, CROW = w5("crow", [P, 2, 4, P])
        braw, BRAW = w5("braw", [P, 2, PAIRS, SH])
        Dg, _ = w5("Dg", [SH, SG])
        drow, _ = w5("drow", [SG, SH])
        dtrow, _ = w5("dtrow", [PAIRS, 2])
        v5, _ = w5("v5", [P, 16, PAIRS])
        Pw, _ = w5("Pw", [P, 2, LC + 1, PAIRS])
        Pr, _ = w5("Pr", [P, 2, LC, PAIRS])
        BB, _ = w5("BB", [P, 2, PAIRS, SH])
        CC, _ = w5("CC", [P, 2, PAIRS, SH])
        AA, _ = w5("AA", [P, PAIRS, 2, 2])
        sc5, _ = w5("sc5", [P, PAIRS, 2, 2])
        XE0, XEO = w5("XE0", [P, BP, 2, P])
        tx, _ = w5("tx", [P, BP, P])
        WE0, WEO = w5("WE0", [P, BP, 2, P])
        tw, _ = w5("tw", [P, BP, (LC + 1) * SH])
        tv, _ = w5("tv", [P, BP, (LC + 1) * SH])
        dtmp, _ = w5("dtmp", [SH, 2 * BP, SH])
        XE = [XE0, at("XE1", [P, BP, 2, P], SQO)]
        WE = [WE0, at("WE1", [P, BP, 2, P], ZUO)]
        WC = [at("WC0", [P, BP, 2, (LC + 1) * SH], XEO), at("WC1", [P, BP, 2, (LC + 1) * SH], SQO)]
        TT = [at("TT0", [P, 2 * BP, P], WEO), at("TT1", [P, 2 * BP, P], ZUO)]
        K16 = [at("K0", [SH, 2 * BP, P], CROW), at("K1", [SH, 2 * BP, P], BRAW)]
        u_dram = nc.dram_tensor("u_scratch", (KD, P, LC, NC5), F32, kind="Internal").ap()
        y_dram = nc.dram_tensor("y_scratch", (KD, P, LC, NC5), F32, kind="Internal").ap()
        yhi, ylo = at("yhi", [P, KD, T2], FREE + 2 * R8, F32R), at("ylo", [P, KD, T2], FREE + 3 * R8, F32R)
        Sg = at("Sg", [P, NB32, P], FREE + 2 * R8)
        QH, KH = at("QH", [P, KD, T2], FREE), at("KH", [P, KD, T2], FREE + 3 * R8)
        VO = FREE + 4 * R8
        Vt = at("Vt", [P, TB2, D], VO)
        ko = at("ko", [P, 4, P], VO + 20480)
        sT = at("sT", [P, TB2, P], VO + 20480 + 4096)
        ex = at("ex", [P, 2, T2], ZUO)
        rmask = at("rmask", [P, T2], ZUO + 8 * T2)
        LF = at("LF", [P, KD, T2], FREE + 2 * R8)
        dec = at("dec", [P, KD, NCK], SQO)
        dec2 = at("dec2", [P, KD, NB32], SQO + 4 * KD * NCK)
        kout = at("kout", [P, T2], RSO)
        yahi, yalo = at("yahi", [P, KD, T2], FREE + 3 * R8, F32R), at("yalo", [P, KD, T2], FREE + R8, F32R)
        ybhi, yblo = at("ybhi", [P, KD, T2], VO, F32R), at("yblo", [P, KD, T2], FREE + 2 * R8, F32R)
        og = at("og", [P, KD, T2], FREE + 2 * R8)
        mrg = at("mrg", [P, KD, T2], FREE)
        gat = at("gat", [P, 2, T2], ZUO)
        orow = at("orow", [P, QB, D], ZREG)

        ps = ctx.enter_context(nc.psum_tensor("ps", [P, 8, 512], F32))

        def const(name, rows=P, n=P):
            return cst[0:rows, CONST[name]:CONST[name] + n]

        def col(name, k=0, rows=slice(0, P)):
            return par[rows, ROW[name] + k:ROW[name] + k + 1]

        def tok(ap, k, T):
            return ap[:, k, META:T2] if T == T1 else ap[:, k, :]

        def halves(T):
            return [(0, 0, T)] if T <= 512 else [(0, 0, HT2), (1, HT2, T)]

        def acc(n, T):
            s = 2 * (n % 2)
            return ps[:, s, 0:T] if T <= 512 else ps[:, s:s + 2, 0:HT2]

        def second(ap):
            return ap.rearrange("p (c r t) -> p c r t", r=2, t=CK)[:, :, 1, :]

        def wide(ap, T):
            return ap if T <= 512 else ap.rearrange("p (a b) -> p a b", a=2)

        s_par2 = sem("s_par2")
        s_xin, s_cst, s_par, s_meta = sem("s_xin"), sem("s_cst"), sem("s_par"), sem("s_meta")
        early_in = [sem(f"early_in{i}") for i in range(PRE)]
        landed = [sem(f"landed{i}") for i in range(NST)]
        hi_done, split_done = sem("hi_done"), sem("split_done")
        marks = sem("marks")
        emptied = [sem(f"emptied{i}") for i in range(2)]
        ada_done, mod_mm, conv_mid = sem("ada_done"), sem("mod_mm"), sem("conv_mid")
        s_silu = sem("s_silu")
        prow_t, par_done = sem("prow_t"), sem("par_done")
        xt_mm, xt_done, meta_t, meta_done = sem("xt_mm"), sem("xt_done"), sem("meta_t"), sem("meta_done")
        sq_done, stat_mm, rs_done = sem("sq_done"), sem("stat_mm"), sem("rs_done")
        zu_done, zhi_done, zlo_done = sem("zu_done"), sem("zhi_done"), sem("zlo_done")
        a_link, v_link, p_link = sem("a_link"), sem("v_link"), sem("p_link")
        tab_ready, tab_done = sem("tab_ready"), sem("tab_done")
        gsq_done, gstat_mm, grs_done = sem("gsq_done"), sem("gstat_mm"), sem("grs_done")
        gq_done, grot_mm, gcos_done, gsin_done, ghead_done = (sem("gq_done"), sem("grot_mm"), sem("gcos_done"),
                                                              sem("gsin_done"), sem("ghead_done"))
        at_s, at_mask, at_neg, at_exp, at_p = sem("at_s"), sem("at_mask"), sem("at_neg"), sem("at_exp"), sem("at_p")
        at_t, at_pt, at_o, mixhi, mixlo = sem("at_t"), sem("at_pt"), sem("at_o"), sem("mixhi"), sem("mixlo")
        conv_done, silu_done, gf_done, ghi_done, glo_done = (sem("conv_done"), sem("silu_done"), sem("gf_done"),
                                                             sem("ghi_done"), sem("glo_done"))
        pads = sem("pads")
        s5_in, s5_turn, s5_vec, s5_bb, s5_tab = sem("s5_in"), sem("s5_turn"), sem("s5_vec"), sem("s5_bb"), sem("s5_tab")
        dt_wide = sem("dt_wide")
        s5_exp, s5_sin = sem("s5_exp"), sem("s5_sin")
        us_out, ys_out = sem("us_out"), sem("ys_out")
        u5_in, xe_done, xe_t, we_done, e_mm, e_done = (sem("u5_in"), sem("xe_done"), sem("xe_t"), sem("we_done"),
                                                       sem("e_mm"), sem("e_done"))
        scan_t, scan_u, scan_done, tt_zero = sem("scan_t"), sem("scan_u"), sem("scan_done"), sem("tt_zero")
        wc_done, k_mm, k_out, k_done, y_mm, y_done = (sem("wc_done"), sem("k_mm"), sem("k_out"), sem("k_done"),
                                                      sem("y_mm"), sem("y_done"))
        tt_in = [sem("tt_in0"), sem("tt_in1")]
        yT_in, gelu_done, yhi_done, ylo_done, ya_done = (sem("yT_in"), sem("gelu_done"), sem("yhi_done"),
                                                         sem("ylo_done"), sem("ya_done"))
        lb_in, lb_sig, lb_done = sem("lb_in"), sem("lb_sig"), sem("lb_done")
        lf_done, cum_done, ep_done, em_done, qin_done, kin_done, dec_done = (
            sem("lf_done"), sem("cum_done"), sem("ep_done"), sem("em_done"), sem("qin_done"), sem("kin_done"),
            sem("dec_done"))
        gsc2_mm, q32_done = sem("gsc2_mm"), sem("q32_done")
        rmask_done, xe_re, wc_re = sem("rmask_done"), sem("xe_re"), sem("wc_re")
        kk_done, kout_done, kt_mm, ko_done = sem("kk_done"), sem("kout_done"), sem("kt_mm"), sem("ko_done")
        gsc_mm, sT_done, dl_mm, st_done, o_mm, o_done = (sem("gsc_mm"), sem("sT_done"), sem("dl_mm"), sem("st_done"),
                                                         sem("o_mm"), sem("o_done"))
        osq_done, ostat_mm, oln_done, ors_done, on_done = (sem("osq_done"), sem("ostat_mm"), sem("oln_done"),
                                                           sem("ors_done"), sem("on_done"))
        og_done, yb_done, ybhi_done, yblo_done, yahi_done, yalo_done = (
            sem("og_done"), sem("yb_done"), sem("ybhi_done"), sem("yblo_done"), sem("yahi_done"), sem("yalo_done"))
        mrg_done, mrghi_done, mrglo_done = sem("mrg_done"), sem("mrghi_done"), sem("mrglo_done")
        fin_done, ot_mm, ot_done, s_out = sem("fin_done"), sem("ot_mm"), sem("ot_done"), sem("s_out")

        class Chain:

            def __init__(self, eng, sm):
                self.eng, self.sm, self.n, self.add = eng, sm, 0, None

            def __call__(self, ins):
                ins.then_inc(self.sm, 1)
                self.n += 1
                self.eng.wait_ge(self.sm, self.n if self.add is None else self.add + self.n)

            def loop(self, i, per):
                self.per, self.start, self.add = per, self.n, i * per

            def end(self, rounds):
                assert self.n - self.start == self.per
                self.n, self.add = self.start + rounds * self.per, None

        def plus(n, i, step):
            return n if i is None else i * step + n

        def wait_emptied(eng, n, i=None, step=4):
            if n >= 2:
                eng.wait_ge(emptied[n % 2], plus(n // 2, i, step // 2))

        def wait_job_out(eng, n, i=None, step=4):
            eng.wait_ge(emptied[n % 2], plus(n // 2 + 1, i, step // 2))

        def wait_residual(eng, name, n):
            wait_job_out(eng, J[name] + n - 2)
            wait_job_out(eng, J[name] + n - 1)

        def lat_src(k):
            return HT[:, 8 + k, :]

        NORMS = [
            dict(src=lambda k: tok(xT, k, T1), K=8, T=T1, gain=lambda k: gsc[:, 0, k:k + 1],
                 shift=lambda k: mod[:, k:k + 1], hi=lambda k: zhi[:, k, 0:T1], lo=lambda k: zlo[:, k, 0:T1]),
            dict(src=lat_src, K=4, T=T1, gain=lambda k: col("g_ql", k), shift=None,
                 hi=lambda k: lhi[:, k, :], lo=lambda k: llo[:, k, :]),
            dict(src=lambda k: lat_src(4 + k), K=2, T=T1, gain=lambda k: col("g_kvl", k), shift=None,
                 hi=lambda k: lhi[:, 4 + k, :], lo=lambda k: llo[:, 4 + k, :]),
            dict(src=lambda k: tok(xT, k, T1), K=8, T=T1, gain=lambda k: gsc[:, 1, k:k + 1],
                 shift=lambda k: mod[:, 24 + k:25 + k], hi=lambda k: zhi[:, k, 0:T1], lo=lambda k: zlo[:, k, 0:T1]),
            dict(src=lambda k: xT[:, k, :], K=8, T=T2, gain=lambda k: col("g_mix2", k), shift=None,
                 hi=lambda k: zhi[:, k, :], lo=lambda k: zlo[:, k, :]),
            dict(src=lambda k: xT[:, k, :], K=8, T=T2, gain=lambda k: col("g_ffn2", k), shift=None,
                 hi=lambda k: zhi[:, k, :], lo=lambda k: zlo[:, k, :]),
            dict(src=lambda k: tok(xT, k, T1), K=8, T=T1, gain=lambda k: col("g_fin", k), shift=None),
        ]
        nbase = [0]
        for s in NORMS:
            nbase.append(nbase[-1] + s["K"])

        GROUPS = [
            dict(tiles=[0, 1, 2, 3], gain=["gdq"] * 4, ones="b64", w=64, rot=True),
            dict(tiles=[4, 5, 6, 7], gain=["gdk"] * 4, ones="b64", w=64, rot=True),
            dict(tiles=[8, 9, 10, 11], gain=["gqn"] * 4, ones="b64", w=64, rot=False),
            dict(tiles=[12, 13, 14, 15], gain=["gkn"] * 4, ones="b64", w=64, rot=False),
            dict(tiles=[16, 17, 18], gain=["gqp", "gqp", "gkp"], ones="b32", w=32, rot=True),
        ]
        RAW = {}
        for name, n, t0 in (("ql", 4, 8), ("kvl", 2, 12), ("kpe", 1, 18), ("dq", 4, 0), ("dk", 4, 4), ("qn01", 2, 8),
                            ("qn23", 2, 10), ("qp", 2, 16), ("kn", 4, 12)):
            for j in range(n):
                RAW[plan.job0[name] + j] = t0 + j
        J, U = plan.job0, plan.unit0
        SCAN_STEPS = NC5 - 2
        TS2 = [0, P, 2 * P, 3 * P, T2 - P]
        STEPS = [(kind, h, i) for kind in ("mla", "dil") for h in range(HEADS) for i in range(QB)]
        NS = len(STEPS)

        FFNS = [dict(T=T1, up="w_up", down="w_down", cw="cw", cb="cb", key="b1", g2=40),
                dict(T=T2, up="w_up_2", down="w_down_2", cw="cw2", cb="cb2", key="b2", g2=None)]
        ROTS = [g for g, s in enumerate(GROUPS) if s["rot"]]
        n_par = sum(1 + ((ROW[n] + k - 1) // P - ROW[n] // P) for n, _, k in PARAMS) + 0
        n_par2 = sum(r for _, _, r in HEAD_PARAMS) + 1

        block = ctx.enter_context(nc.Block())

        def kpn(ap):
            return ap.rearrange("(k p) n -> p k n", p=P)

        w_ada, w_in, w_qb, w_kvb, w_o = (kpn(A[n][0]) for n in ("w_ada", "w_in", "w_q_b", "w_kv_b", "w_o"))

        def unit_views(name, j):
            def whole(src, k=KD, c=P):
                return [(lambda s: s[:, 0:k * c].rearrange("p (k c) -> p k c", k=k), src)]

            if name == "ada":
                return [(lambda s: s[:], w_ada[:, j % KD, j // KD * D:(j // KD + 1) * D])]
            if name in ("ql", "kvl"):
                c0 = (0 if name == "ql" else QL) + j * P
                return whole(w_in[:, :, c0:c0 + P])
            if name == "kpe":
                return [(lambda s, r=r: s[:].rearrange("p (k r c) -> p k r c", k=KD, r=4)[:, :, r, :],
                         w_in[:, :, QL + KVL:QL + KVL + RD]) for r in range(4)]
            if name in ("dq", "dk"):
                c0 = QL + KVL + RD + (0 if name == "dq" else 512) + j * P
                return whole(w_in[:, :, c0:c0 + P])
            if name == "dv":
                c0 = QL + KVL + RD + 1024
                return whole(w_in[:, 2 * j:2 * j + 2, c0:c0 + 512], 2, 512)
            if name in ("qn01", "qn23", "qp"):
                v = w_qb.rearrange("p k (h c) -> p k h c", c=HD + RD)
                res = []
                for t in range(2):
                    for k in range(4):
                        if name == "qp":
                            src = v[:, k, 4 * t:4 * t + 4, HD:HD + RD]
                        else:
                            h = 2 * (t + 2 * (name == "qn23"))
                            src = v[:, k, h:h + 2, 0:HD]
                        n = src.shape[1]
                        res.append((lambda s, o=(4 * t + k) * P, n=n: s[:, o:o + P].rearrange("p (h c) -> p h c", h=n), src))
                return res
            v = w_kvb.rearrange("p k (h c) -> p k h c", c=2 * HD)
            if name == "kn":
                return [(lambda s, o=(2 * t + k) * P: s[:, o:o + P].rearrange("p (h c) -> p h c", h=2),
                         v[:, k, 2 * t:2 * t + 2, 0:HD]) for t in range(4) for k in range(2)]
            if name == "mv":
                return [(lambda s, o=k * 512: s[:, o:o + 512].rearrange("p (h c) -> p h c", h=8),
                         v[:, k, :, HD:2 * HD]) for k in range(2)]
            raise KeyError(name)

        def stage_free(eng, n, i=None, step=4):
            if n < NST:
                return
            kind, m, _ = plan.loads[n - NST]
            eng.wait_ge(ada_done if kind == "ada" else split_done, plus(m + 1 + (PRE if kind == "ada" else 0), i, step))

        def load_unit(eng, n, views):
            stage_free(eng, n)
            for part, src in views:
                eng.dma_start(part(stage[n % NST]), src).then_inc(landed[n % NST], 16)

        def stream(eng, n0, count, view):
            stream_first(eng, n0, view)
            stream_rest(eng, n0, count, view)

        def stream_first(eng, n0, view):
            for j in range(4):
                load_unit(eng, n0 + j, [(lambda s, k=view(0, j).shape[1], c=view(0, j).shape[2]:
                                         s[:, 0:k * c].rearrange("p (k c) -> p k c", k=k), view(0, j))])

        def stream_rest(eng, n0, count, view):
            assert count % 4 == 0
            if count == 4:
                return
            with eng.Fori(0, count // 4 - 1) as i:
                for j in range(4):
                    n = n0 + j
                    eng.wait_ge(split_done, i * 4 + (plan.loads[n + 4 - NST][1] + 1))
                    src = view(i, j + 4)
                    k, c = src.shape[1], src.shape[2]
                    eng.dma_start(stage[n % NST][:, 0:k * c].rearrange("p (k c) -> p k c", k=k), src)\
                       .then_inc(landed[n % NST], 16)

        def ffn_loads(eng, f):
            up, down = kpn(A[f["up"]][0]), kpn(A[f["down"]][0])
            for kind, c, n in FFN_ORDER:
                n0 = plan.w_load[U[f["key"] + kind + str(c)]]
                if kind == "up":
                    def view(i, j, c=c):
                        col0 = (8 * c + j // 2) * P + (FF if j % 2 else 0)
                        return up[:, :, bass.ds(i * 2 * P + col0, P)]
                else:
                    def view(i, j, c=c):
                        return down[:, 8 * c:8 * c + CH[c], bass.ds(i * 4 * P + j * P, P)]
                stream(eng, n0, n, view)

        @block.sync
        def _(sp):
            for t in range(QB):
                sp.dma_start(xrow[:, t, :], A["x"][0, t * P:(t + 1) * P, :]).then_inc(s_xin, 16)
            sp.dma_start(cst[:, :], A["consts"]).then_inc(s_cst, 16)
            for a in range(PRE):
                sp.dma_start(early[a][:, :], unit_views("ada", a)[0][1]).then_inc(early_in[a], 16)
            n = 0
            for j in range(PRE, 16):
                load_unit(sp, n, unit_views("ada", j))
                n += 1
            for name, count in ( ("ql", 4), ("kvl", 2), ("kpe", 1), ("dq", 4), ("dk", 4), ("dv", 4),
                                ("qn01", 1), ("qn23", 1), ("qp", 1), ("kn", 1), ("mv", 1)):
                for j in range(count):
                    load_unit(sp, n, unit_views(name, j))
                    n += 1
            for j in range(32):
                load_unit(sp, n, unit_views("ada", 16 + j))
                n += 1
            stream(sp, n, 8, lambda i, j: w_o[:, :, bass.ds(i * 4 * P + j * P, P)])
            ffn_loads(sp, FFNS[0])
            w_in2 = kpn(A["w_in_2"][0])

            def cols(src, c0):
                return lambda i, j: src[:, :, bass.ds(i * 4 * P + (j * P + c0), P)]

            for k in range(-4, KD):
                unit = plan.w_load[U["u"]] + k + 4
                load_unit(sp, unit, [(lambda s: s[:].rearrange("p (k c) -> p k c", k=KD),
                                      w_in2[:, :, (k + 4) * P:(k + 5) * P])])
                if k >= 0:
                    sp.wait_ge(us_out, 16 * (k + 1))
                    u_view = u_dram[k].rearrange("(g h) j c -> j h g c", h=SH)
                    for j in range(LC):
                        sp.dma_start(U5[SH * j:SH * j + SH, 8 * k:8 * k + 8, :], u_view[j]).then_inc(u5_in, 16)
            stream_rest(sp, plan.w_load[U["q"]], 8, cols(w_in2, 1024))
            glu = cols(kpn(A["ssm_w_glu_2"][0]), 0)
            stream_first(sp, plan.w_load[U["glu"]], glu)

            def y_store(b):
                sp.wait_ge(y_done, b + 1)
                y_view = y_dram[b].rearrange("(g h) j c -> j h g c", h=SH)
                for j in range(LC):
                    sp.dma_start(y_view[j], Y5[SH * j:SH * j + SH, 8 * b:8 * b + 8, :]).then_inc(ys_out, 16)

            for b in range(NB5):
                sp.wait_ge(k_done, b + 1)
                sp.wait_ge(tt_zero, 1)
                if b >= 2:
                    sp.wait_ge(y_mm, b - 1)
                for j in range(LC):
                    sp.dma_start(TT[b % 2][SH * j:SH * j + SH, :, SH * j:P], K16[b % 2][:, :, 0:P - SH * j])\
                      .then_inc(tt_in[b % 2], 16)
                if b >= 2:
                    y_store(b - 2)
            for b in range(NB5 - 2, NB5):
                y_store(b)
            sp.wait_ge(ys_out, 16 * LC * KD)
            sp.wait_ge(y_mm, NB5)
            for k in range(KD):
                sp.dma_start(yT[:, k, :, :], y_dram[k]).then_inc(yT_in, 16)
            stream_rest(sp, plan.w_load[U["glu"]], 8, glu)
            stream(sp, plan.w_load[U["f"]], 8, cols(w_in2, 2048))
            for half in range(2):
                for j in range(4):
                    load_unit(sp, plan.w_load[U["i%d" % half] + j],
                              [(lambda s: s[:].rearrange("p (k c) -> p k c", k=2),
                                w_in2[:, 2 * j:2 * j + 2, 3072 + 512 * half:3584 + 512 * half])])
            stream(sp, plan.w_load[U["og"]], 8, cols(w_in2, 4096))
            wsp, whp = kpn(A["w_ssm_proj_2"][0]), kpn(A["w_hgrn_proj_2"][0])

            def merge_view(i, j):
                src, c0 = ((w_in2, 5120), (wsp, 0), (w_in2, 6144), (whp, 0))[j % 4]
                return src[:, :, bass.ds(i * P + (c0 + j // 4 * P), P)]

            stream(sp, plan.w_load[U["mrg"]], 32, merge_view)
            stream(sp, plan.w_load[U["out"]], 8, cols(kpn(A["w_out_2"][0]), 0))
            ffn_loads(sp, FFNS[1])
            for t in range(QB):
                sp.wait_ge(ot_done, 2 * t + 2)
                sp.dma_start(out[0, t * P:(t + 1) * P, :], orow[:, t, :]).then_inc(s_out, 16)
            sp.wait_ge(s_out, 16 * QB)

        @block.scalar
        def _(act):
            link = Chain(act, a_link)

            def split_hi(u, i=None, step=4):
                slot, value = plan.landed[plan.w_load[u]]
                act.wait_ge(landed[slot], plus(value, i, 16 * step // NST))
                if u >= NHL:
                    act.wait_ge(marks, plus(plan.free[u - NHL], i, step))
                act.activation(whi[u % NHL][:], stage[slot][:], ACT.Copy).then_inc(hi_done, 1)

            def norm(n, units={}):
                s = NORMS[n]
                K, T, b = s["K"], s["T"], nbase[n]
                for k in range(K):
                    if b + k >= 2:
                        act.wait_ge(stat_mm, b + k - 1)
                    act.activation(sq[:, (b + k) % 2, 0:T], s["src"](k), ACT.Square).then_inc(sq_done, 1)
                act.wait_ge(stat_mm, b + K)
                if n:
                    act.wait_ge(zu_done, b)
                stat = ps[:, 4, 0:T] if T <= 512 else ps[:, 4:6, 0:HT2]
                link(act.activation(wide(rs[:, 0:T], T), stat, ACT.Ln, scale=1.0 / (K * P), bias=small[:, 0:1]))
                act.activation(rs[:, 0:T], rs[:, 0:T], ACT.Exp, scale=-0.5).then_inc(rs_done, 1)
                for k in range(K if "hi" in s else 0):
                    act.wait_ge(zu_done, b + k + 1)
                    act.activation(s["hi"](k), zu[:, (b + k) % NZU, 0:T], ACT.Identity,
                                   bias=s["shift"](k) if s["shift"] else 0.0).then_inc(zhi_done, 1)
                    if k in units:
                        split_hi(units[k])

            for name, src, k in PARAMS:
                flat = A[src].rearrange("a b c -> (a b c)" if len(A[src].shape) == 3 else
                                        "a b -> (a b)" if len(A[src].shape) == 2 else "a -> a")
                v, r0, done = flat.rearrange("(r c) -> r c", c=P), ROW[name], 0
                while done < k:
                    b, p0 = divmod(r0 + done, P)
                    m = min(k - done, P - p0)
                    act.dma_start(prow[p0:p0 + m, b, :], v[done:done + m, :]).then_inc(s_par, 16)
                    done += m
            act.wait_ge(par_done, 1)
            act.activation(csil[:, :], par[:, ROW["c"]:ROW["c"] + 8], ACT.Silu).then_inc(s_silu, 1)
            for k in range(KD):
                act.wait_ge(xt_mm, k + 1)
                act.activation(xT[:, k, META:T2], ps[:, 5 + k % 2, :], ACT.Copy).then_inc(xt_done, 1)
            act.wait_ge(xt_done, KD)
            act.wait_ge(pads, 1)
            norm(0, {2: 0, 4: 1, 6: 2})

            def raw_jobs(name, n, ahead=None):
                for j in range(n):
                    job = J[name] + j
                    if ahead is not None:
                        split_hi(ahead + j)
                    act.wait_ge(marks, plan.full[job])
                    act.activation(HT[:, RAW[job], :], acc(job, T1), ACT.Copy).then_inc(emptied[job % 2], 1)

            raw_jobs("ql", 4, U["ql"] + 3)
            raw_jobs("kvl", 2, U["kvl"] + 3)
            norm(1)
            norm(2)
            act.wait_ge(tab_ready, 2)
            act.activation(tab[:, :, :], tab[:, :, :], ACT.Sin).then_inc(tab_done, 1)
            raw_jobs("kpe", 1, U["kpe"] + 3)
            raw_jobs("dq", 4, U["dq"] + 3)
            raw_jobs("dk", 4, U["dk"] + 3)
            split_hi(U["dv"] + 3)
            for j in range(QB):
                job = J["dv"] + j
                act.wait_ge(marks, plan.full[job])
                act.activation(Vd[:, j, :], acc(job, T1), ACT.Copy).then_inc(emptied[job % 2], 1)
            for u in range(3):
                split_hi(U["qn01"] + u)

            def group(g):
                s = GROUPS[g]
                n, t0 = len(s["tiles"]), s["tiles"][0]
                if g >= 2:
                    act.wait_ge(ghead_done, g - 1)
                act.activation(sqg[g % 2][:, 0:n, :], HT[:, t0:t0 + n, :], ACT.Square).then_inc(gsq_done, 1)
                act.wait_ge(gstat_mm, g + 1)
                link(act.activation(sqg[g % 2][:, 0:n, :], ps[:, 4:4 + n, :], ACT.Ln,
                                    scale=1.0 / s["w"], bias=small[:, 0:1]))
                act.activation(sqg[g % 2][:, 0:n, :], sqg[g % 2][:, 0:n, :], ACT.Exp, scale=-0.5).then_inc(grs_done, 1)

            wait_job_out(act, J["dk"] + 2)
            wait_job_out(act, J["dk"] + 3)
            group(0)
            raw_jobs("qn01", 2)
            split_hi(U["kn"])
            raw_jobs("qn23", 2)
            split_hi(U["mv"])
            group(1)
            raw_jobs("qp", 2)
            raw_jobs("kn", 4)
            for j in range(QB):
                job = J["mv"] + j
                act.wait_ge(marks, plan.full[job])
                act.activation(Vm[:, j, :], acc(job, T1), ACT.Copy).then_inc(emptied[job % 2], 1)
            wait_job_out(act, J["mv"] + 2)
            wait_job_out(act, J["mv"] + 3)
            for g in range(2, 5):
                group(g)
            for t in range(NS + 3):
                if t < NS:
                    kind, h, i = STEPS[t]
                    w = (i + 1) * P
                    act.wait_ge(at_neg, t + 1)
                    act.activation(pb[:, t % 4, 0:w], pb[:, t % 4, 0:w], ACT.Exp, bias=small[:, 8 + t % 4:9 + t % 4],
                                   accum_out=small[:, 12 + t % 4:13 + t % 4]).then_inc(at_exp, 1)
                if 2 <= t < NS + 2:
                    q = t - 2
                    kind, h, i = STEPS[q]
                    act.wait_ge(at_t, q + 1)
                    if q >= 3:
                        act.wait_ge(at_o, q - 2)
                    act.activation(PT[:, q % 3, 0:(i + 1) * P], ps[:, 2 + q % 2, 0:(i + 1) * P], ACT.Copy)\
                       .then_inc(at_pt, 1)
                if t >= 3 and (t - 3) % 8 == 7:
                    m = (t - 3) // 8
                    act.wait_ge(at_o, 8 * m + 8)
                    act.activation(mhi[:, m, :], ps[:, 4 + m % 2, :], ACT.Copy).then_inc(mixhi, 1)
            for u in range(3):
                split_hi(U["wo"] + u)
            with act.Fori(0, 2) as i:
                for j in range(4):
                    split_hi(U["wo"] + 3 + j, i)
            wait_residual(act, "wo", 8)
            norm(3)

            def ffn(b):
                f = FFNS[b]
                T, key = f["T"], f["key"]
                for kind, c, n in FFN_ORDER:
                    job0, u0 = J[key + kind + str(c)], U[key + kind + str(c)]
                    last = b == len(FFNS) - 1 and (kind, c) == ("down", 2)
                    rounds = n // 4
                    pair0 = 22 * b + 8 * c
                    with act.Fori(0, rounds - (1 if last else 0)) as i:
                        for j in range(4):
                            split_hi(u0 + 3 + j, i)
                            if kind == "up":
                                up_job(f, c, job0, pair0, i, j)
                    if last:
                        split_hi(u0 + n - 1)

            def up_job(f, c, job0, pair0, i, j):
                T, job = f["T"], job0 + j
                act.wait_ge(marks, plus(plan.full[job], i, 4))
                cj = 2 * pair0 + j
                if cj >= 2:
                    act.wait_ge(conv_done, i * 4 + cj)
                else:
                    act.wait_ge(conv_done, i * 4 + 1)
                act.activation(wide(ub[:, j % 2, 2:2 + T], T), acc(job, T), ACT.Copy).then_inc(emptied[job % 2], 1)
                if j % 2:
                    q = j // 2
                    act.wait_ge(conv_done, i * 4 + (cj + 1))
                    act.activation(cv[:, q, 0, 0:T], cv[:, q, 0, 0:T], ACT.Silu).then_inc(silu_done, 1)
                    act.wait_ge(gf_done, i * 2 + (pair0 + q + 1))
                    if c == 2:
                        act.wait_ge(marks, plan.full[J[f["key"] + "down0"] + 7])
                    elif f["key"] != "b1":
                        act.wait_ge(marks, plan.full[J["b1down2"] + 7])
                    act.activation(ghi[c % 2][:, bass.ds(i * 2 + q, 1), 0:T].rearrange("p a t -> p (a t)"),
                                   cv[:, q, 1, 0:T], ACT.Copy).then_inc(ghi_done, 1)

            ffn(0)

            wait_residual(act, "b1down2", 8)
            norm(4)
            def u_job(j):
                split_hi(U["u"] + 3 + j)
                job = J["u"] + j
                act.wait_ge(marks, plan.full[job])
                for b in range(2):
                    ins = act.activation(uD[:, j, :, b * NC5 // 2:(b + 1) * NC5 // 2],
                                         ps[:, 2 * (job % 2) + b, 0:HT2].rearrange("p (c j) -> p j c", j=LC), ACT.Copy)
                ins.then_inc(emptied[job % 2], 1)

            for j in range(4):
                u_job(j)
            act.wait_ge(s5_vec, 1)
            act.activation(v5[:, 2, :], v5[:, 2, :], ACT.Exp).then_inc(s5_exp, 1)
            act.wait_ge(s5_vec, 2)
            act.activation(v5[:, 3, :], v5[:, 3, :], ACT.Exp).then_inc(s5_exp, 1)
            act.wait_ge(s5_vec, 3)
            act.activation(v5[:, 7:9, :], v5[:, 7:9, :], ACT.Sin).then_inc(s5_sin, 1)
            act.wait_ge(lb_in, 1)
            act.activation(gsc[:, 2, :], gsc[:, 2, :], ACT.Sigmoid).then_inc(lb_sig, 1)
            for j in range(4, 8):
                u_job(j)
            for b in range(NB5):
                act.wait_ge(xe_t, b + 1)
                if b >= 2:
                    act.wait_ge(e_mm, b - 1)
                act.activation(WE[b % 2][:, :, :, :].rearrange("p q c k -> p (q c k)").rearrange("p (b k) -> p b k", b=2),
                               ps[:, 6:8, :], ACT.Copy).then_inc(we_done, 1)

            def k_evac(b):
                act.wait_ge(k_mm, b + 1)
                if b >= 2:
                    act.wait_ge(tt_in[b % 2], 16 * LC * (b // 2))
                act.activation(K16[b % 2][:, :, :].rearrange("p (q r) k -> p r q k", r=2),
                               ps[0:SH, 6:8, :].rearrange("p r (q k) -> p r q k", k=P), ACT.Copy).then_inc(k_out, 1)

            def evac(name, j, i, fn, out):
                n = J[name] + j
                act.wait_ge(marks, plus(plan.full[n], i, 4))
                act.activation(wide(out, T2), acc(n, T2), fn).then_inc(emptied[n % 2], 1)

            k_evac(0)
            act.wait_ge(us_out, 16 * KD)
            with act.Fori(0, 2) as i:
                for j in range(4):
                    split_hi(U["q"] + 3 + j, i)
                    evac("q", j, i, ACT.Copy, QH[:, bass.ds(i * 4 + j, 1), :].rearrange("p a t -> p (a t)"))
            for b in range(NB5):
                if b + 1 < NB5:
                    k_evac(b + 1)
                act.wait_ge(y_mm, b + 1)
                act.activation(Y5[:, 8 * b:8 * b + 8, :].rearrange("p (q r) c -> p r q c", r=2),
                               ps[:, 4:6, 0:4 * NC5].rearrange("p r (q c) -> p r q c", c=NC5), ACT.Copy).then_inc(y_done, 1)
            act.wait_ge(yT_in, 16 * KD)
            for k in range(KD):
                act.activation(y5[:, k, :].rearrange("p (c j) -> p j c", j=LC), yT[:, k, :, :],
                               ACT.Gelu_apprx_tanh).then_inc(gelu_done, 1)
                act.wait_ge(gelu_done, k + 1)
                act.activation(yhi[:, k, :], y5[:, k, :], ACT.Copy).then_inc(yhi_done, 1)

            with act.Fori(0, 2) as i:
                for j in range(4):
                    split_hi(U["glu"] + 3 + j, i)
                    act.wait_ge(ya_done, plus(max(j - 1, 0) + 1, i, 4))
                    evac("glu", j, i, ACT.Sigmoid, gat[:, j % 2, :])
            for j in range(8):
                split_hi(U["f"] + 3 + j)
                evac("f", j, None, ACT.Sigmoid, KH[:, j, :])
            split_hi(U["i0"] + 3)
            act.wait_ge(lb_done, 1)
            wait_residual(act, "f", 8)
            for h in range(HEADS):
                act.activation(LF[:, h, :], KH[:, h, :], ACT.Ln, scale=gsc[:, 3, h:h + 1],
                               bias=gsc[:, 2, h:h + 1]).then_inc(lf_done, 1)

            def gate_exps(h):
                act.wait_ge(cum_done, h + 1)
                if h >= 2:
                    act.wait_ge(dec_done, h - 1)
                act.activation(ex[:, h % 2, :], LF[:, h, :], ACT.Exp).then_inc(ep_done, 1)
                act.wait_ge(ep_done, h + 1)
                act.activation(LF[:, h, :], LF[:, h, :], ACT.Exp, scale=-1.0).then_inc(em_done, 1)

            for half in range(2):
                for j in range(TB2):
                    n = J["i%d" % half] + j
                    act.wait_ge(marks, plan.full[n])
                    act.activation(Vt[:, j, half * 512:(half + 1) * 512], ps[:, 2 * (n % 2), 0:512], ACT.Copy)\
                       .then_inc(emptied[n % 2], 1)
                    if half * 4 + j < (4 if half == 0 else HEADS):
                        gate_exps(half * 4 + j)
                if half == 0:
                    for u in range(4):
                        split_hi(U["i1"] + u)
            for u in range(3):
                split_hi(U["og"] + u)

            def k_out_evac(h):
                act.wait_ge(kt_mm, h + 1)
                if h:
                    act.wait_ge(dl_mm, NB32 * h)
                act.activation(ko[:, :, :].rearrange("p b d -> p (b d)"), ps[:, 5, :], ACT.Copy).then_inc(ko_done, 1)

            k_out_evac(0)
            for h in range(HEADS):
                if h + 1 < HEADS:
                    k_out_evac(h + 1)
                act.wait_ge(o_mm, h + 1)
                act.activation(QH[:, h, 0:256], ps[:, 6, 0:256], ACT.Copy)
                act.activation(QH[:, h, 256:T2], ps[:, 7, 0:272], ACT.Copy).then_inc(o_done, 1)
            act.wait_ge(o_done, HEADS)
            for h in range(HEADS):
                act.activation(KH[:, h, :], QH[:, h, :], ACT.Square).then_inc(osq_done, 1)

            def og_job(j):
                split_hi(U["og"] + 3 + j)
                evac("og", j, None, ACT.Silu, og[:, j, :])

            for j in range(4):
                og_job(j)
            for h in range(HEADS):
                act.wait_ge(ostat_mm, h + 1)
                act.activation(wide(KH[:, h, :], T2), ps[:, 4 + 2 * (h % 2):6 + 2 * (h % 2), 0:HT2], ACT.Ln,
                               scale=1.0 / P, bias=small[:, 0:1]).then_inc(oln_done, 1)
            act.wait_ge(oln_done, HEADS)
            for h in range(HEADS):
                act.activation(KH[:, h, :], KH[:, h, :], ACT.Exp, scale=-0.5).then_inc(ors_done, 1)
            for j in range(4, 8):
                og_job(j)
                act.wait_ge(on_done, HEADS)
                for k in (2 * j - 8, 2 * j - 7):
                    act.activation(yahi[:, k, :], y5[:, k, :], ACT.Copy).then_inc(yahi_done, 1)
            for k in range(KD):
                act.wait_ge(og_done, k + 2)
                act.activation(ybhi[:, k, :], QH[:, k, :], ACT.Copy).then_inc(ybhi_done, 1)
            with act.Fori(0, 8) as i:
                for j in range(4):
                    split_hi(U["mrg"] + 3 + j, i)
                    if j % 2 == 0:
                        act.wait_ge(mrg_done, plus(1, i, 1))
                        evac("mrg", j, i, ACT.Sigmoid, gat[:, j // 2, :])
            act.wait_ge(mrg_done, KD + 1)
            for k in range(KD):
                act.activation(zhi[:, k, :], mrg[:, k, :], ACT.Copy).then_inc(mrghi_done, 1)
            with act.Fori(0, 2) as i:
                for j in range(4):
                    split_hi(U["out"] + 3 + j, i)
            wait_residual(act, "out", 8)
            norm(5)
            ffn(1)
            wait_residual(act, "b2down2", 8)
            norm(6)
            for t in range(QB):
                for half in range(2):
                    n = 2 * t + half
                    act.wait_ge(ot_mm, n + 1)
                    act.activation(orow[:, t, half * 512:(half + 1) * 512], ps[:, 6 + n % 2, :], ACT.Copy)\
                       .then_inc(ot_done, 1)

        @block.tensor
        def _(pe):
            def job(n, u, lhs_rhs, T, last_i=None, i=None):
                pass

            def products(n, T, ks, w, x_hi, x_lo, fresh=None):
                last = None
                for b, t0, t1 in halves(T):
                    out = ps[:, 2 * (n % 2) + b, 0:t1 - t0]
                    for k in range(ks):
                        if fresh and b == 0:
                            pe.wait_ge(fresh[0], fresh[1] + k + 1)
                        for a, x in ((whi, x_hi), (whi, x_lo), (wlo, x_hi)):
                            last = pe.matmul(out, w(a, k), x(k, t0, t1), start=(k == 0 and a is whi and x is x_hi),
                                             stop=(k == ks - 1 and a is wlo))
                return last

            def gemm(name, j, x_hi, x_lo, T, ks=KD, i=None, fresh=None):
                n, u = J[name] + j, U[name] + j
                pe.wait_ge(split_done, plus(u + 1, i, 4))
                wait_emptied(pe, n, i)
                products(n, T, ks, lambda a, k: a[u % NHL][:, k * P:(k + 1) * P], x_hi, x_lo, fresh)\
                    .then_inc(marks, 1)

            def zx(part):
                return lambda k, a, b: part[:, k, a:b]

            pe.wait_ge(s_cst, 16)
            pe.wait_ge(s_par, 16 * n_par)
            pe.wait_ge(s_par2, 16 * n_par2)
            for b in range(NBLK):
                r = min(P, NROWS - b * P)
                mm = pe.transpose(ps[:, 4, b * P:b * P + r], prow[0:r, b, :], const("ident", r, r))
            mm.then_inc(prow_t, 1)
            pe.wait_ge(s_xin, 16 * QB)
            for k in range(KD):
                if k >= 2:
                    pe.wait_ge(xt_done, k - 1)
                for t in range(QB):
                    mm = pe.transpose(ps[:, 5 + k % 2, t * P:(t + 1) * P], xrow[:, t, k * P:(k + 1) * P], const("ident"))
                mm.then_inc(xt_mm, 1)
            pe.wait_ge(s_meta, 16)
            for k in range(KD):
                mm = pe.transpose(ps[:, 7, k * META:(k + 1) * META], metar[:, k * P:(k + 1) * P],
                                  const("ident", META, META))
            mm.then_inc(meta_t, 1)

            def norm_stats(n):
                s = NORMS[n]
                for k in range(s["K"]):
                    pe.wait_ge(sq_done, nbase[n] + k + 1)
                    for b, t0, t1 in halves(s["T"]):
                        mm = pe.matmul(ps[:, 4 + b, 0:t1 - t0], const("ones"), sq[:, (nbase[n] + k) % 2, t0:t1],
                                       start=k == 0, stop=k == s["K"] - 1)
                    mm.then_inc(stat_mm, 1)

            def ada_sums(g):
                pe.wait_ge(ada_done, KD * (g + 1))
                for k in range(KD):
                    a = KD * g + k
                    mm = pe.matmul(ps[:, 7, 128 + a:129 + a], asum[g % 2][:, k * P:(k + 1) * P], const("ones", n=1),
                                   start=True, stop=True)
                mm.then_inc(mod_mm, 1)

            pe.wait_ge(par_done, 1)
            pe.wait_ge(xt_done, KD)
            norm_stats(0)
            pe.wait_ge(meta_done, 1)
            for g in range(2):
                ada_sums(g)

            for j in range(4):
                gemm("ql", j, zx(zhi), zx(zlo), T1, fresh=(zlo_done, 0) if j == 0 else None)
            for j in range(2):
                gemm("kvl", j, zx(zhi), zx(zlo), T1)
            gemm("kpe", 0, zx(zhi), zx(zlo), T1)
            norm_stats(1)
            norm_stats(2)
            for j in range(4):
                gemm("dq", j, zx(zhi), zx(zlo), T1)
            for j in range(4):
                gemm("dk", j, zx(zhi), zx(zlo), T1)

            def tokens_out(name, units, jobs, xh, xl, ks, kw, starts=TS2):
                for j in range(jobs):
                    n = J[name] + j
                    wait_emptied(pe, n)
                    out = ps[:, 2 * (n % 2), 0:512]
                    for k in range(ks):
                        uu, o = (U[name] + k // kw) % NHL, (k % kw) * 512
                        if j == 0 and k % kw == 0:
                            pe.wait_ge(split_done, U[name] + k // kw + 1)
                        for a, x in ((whi, xh), (wlo, xh), (whi, xl)):
                            mm = pe.matmul(out, x(k, starts[j], starts[j] + P), a[uu][:, o:o + 512],
                                           start=(k == 0 and a is whi and x is xh), stop=(k == ks - 1 and x is xl))
                    mm.then_inc(marks, 1)

            tokens_out("dv", 4, QB, zx(zhi), zx(zlo), KD, 2)

            def group_stats(g):
                s = GROUPS[g]
                pe.wait_ge(gsq_done, g + 1)
                if g == 0:
                    pe.wait_ge(rs_done, 3)
                elif GROUPS[g - 1]["rot"]:
                    pe.wait_ge(gsin_done, g)
                else:
                    pe.wait_ge(grs_done, g)
                for m in range(len(s["tiles"])):
                    mm = pe.matmul(ps[:, 4 + m, :], const(s["ones"]), sqg[g % 2][:, m, :], start=True, stop=True)
                mm.then_inc(gstat_mm, 1)

            def group_rot(g):
                s = GROUPS[g]
                pe.wait_ge(gq_done, ROTS.index(g) + 1)
                for m, t in enumerate(s["tiles"]):
                    mm = pe.matmul(ps[:, 4 + m, :], const("r%d" % s["w"]), HT[:, t, :], start=True, stop=True)
                mm.then_inc(grot_mm, 1)

            lat = (zx(lhi), zx(llo))
            kvl = tuple((lambda k, a, b, q=q: q[:, 4 + k, a:b]) for q in (lhi, llo))
            group_stats(0)
            pe.wait_ge(zlo_done, nbase[3])

            def several(name, j, ks, x):
                n, u = J[name] + j, U[name]
                pe.wait_ge(split_done, u + 1)
                wait_emptied(pe, n)
                products(n, T1, ks, lambda a, k: a[u % NHL][:, (ks * j + k) * P:(ks * j + k + 1) * P], *x)\
                    .then_inc(marks, 1)

            for name in ("qn01", "qn23"):
                for j in range(2):
                    several(name, j, 4, lat)
            group_rot(0)
            group_stats(1)
            for j in range(2):
                several("qp", j, 4, lat)
            for j in range(4):
                several("kn", j, 2, kvl)
            group_rot(1)
            tokens_out("mv", 1, QB, *kvl, 2, 2)
            group_stats(2)
            group_stats(3)
            group_stats(4)
            group_rot(4)

            def scores(q):
                kind, h, i = STEPS[q]
                if q >= 2:
                    pe.wait_ge(at_mask, q - 1)
                out = ps[:, q % 2, 0:(i + 1) * P]
                t, c = slice(i * P, (i + 1) * P), slice(0, (i + 1) * P)
                r = slice(HD * (h % 2), HD * (h % 2) + HD)
                if kind == "dil":
                    mm = pe.matmul(out, HT[r, h // 2, t], HT[r, 4 + h // 2, c], start=True, stop=True)
                else:
                    pe.matmul(out, HT[r, 8 + h // 2, t], HT[r, 12 + h // 2, c], start=True, stop=False)
                    r = slice(RD * (h % 4), RD * (h % 4) + RD)
                    mm = pe.matmul(out, HT[r, 16 + h // 4, t], HT[r, 18, c], start=False, stop=True)
                mm.then_inc(at_s, 1)

            def turn(q):
                i = STEPS[q][2]
                pe.wait_ge(at_p, q + 1)
                if q >= 2:
                    pe.wait_ge(at_pt, q - 1)
                for j in range(i + 1):
                    mm = pe.transpose(ps[:, 2 + q % 2, j * P:(j + 1) * P], pb[:, q % 4, j * P:(j + 1) * P], const("ident"))
                mm.then_inc(at_t, 1)

            def values(q):
                kind, h, i = STEPS[q]
                V = Vm if kind == "mla" else Vd
                m = q // 8
                pe.wait_ge(at_pt, q + 1)
                if q % 8 == 0 and m >= 2:
                    pe.wait_ge(mixlo, m - 1)
                for j in range(i + 1):
                    mm = pe.matmul(ps[HD * (h % 2):HD * (h % 2) + HD, 4 + m % 2, i * P:(i + 1) * P],
                                   V[:, j, h * HD:(h + 1) * HD], PT[:, q % 3, j * P:(j + 1) * P],
                                   start=j == 0, stop=j == i)
                mm.then_inc(at_o, 1)

            pe.wait_ge(ghead_done, 5)
            wait_job_out(pe, J["mv"] + 2)
            wait_job_out(pe, J["mv"] + 3)
            for t in range(NS + 3):
                if t < NS:
                    scores(t)
                if t >= 18 and t % 16 == 2:
                    ada_sums(1 + t // 16)
                if 2 <= t < NS + 2:
                    turn(t - 2)
                if t >= 3:
                    values(t - 3)

            pe.wait_ge(mixlo, 8)
            with pe.Fori(0, 2) as i:
                for j in range(4):
                    gemm("wo", j, zx(mhi), zx(mlo), T1, i=i)
            norm_stats(3)

            def ffn(b):
                f = FFNS[b]
                T = f["T"]
                for kind, c, n in FFN_ORDER:
                    name = f["key"] + kind + str(c)
                    if kind == "down":
                        pe.wait_ge(glo_done, NF * b + min(8 * c + 8, NF) + 1)
                    with pe.Fori(0, n // 4) as i:
                        for j in range(4):
                            if kind == "up":
                                gemm(name, j, zx(zhi), zx(zlo), T, i=i,
                                     fresh=(zlo_done, nbase[5 if b else 3]) if (c, j) == (0, 0) else None)
                            else:
                                gemm(name, j, zx(ghi[c % 2]), zx(glo[c % 2]), T, ks=CH[c], i=i)

            ffn(0)

            norm_stats(4)
            for j in range(4):
                gemm("u", j, zx(zhi), zx(zlo), T2, fresh=(zlo_done, nbase[4]) if j == 0 else None)
            pe.wait_ge(s5_in, 16 * 22)
            pe.wait_ge(dt_wide, 1)
            for c in range(3):
                pe.transpose(ps[:, 6, c * PAIRS:(c + 1) * PAIRS], s5row[:, c, :], const("ident", PAIRS, PAIRS))
            pe.transpose(ps[0:SH, 6, 3 * PAIRS:3 * PAIRS + SG], drow[:, :], const("ident", SG, SG))
            for c in range(2):
                for o in range(4):
                    mm = pe.transpose(ps[:, 7 - 3 * c, o * P:(o + 1) * P], crow[:, c, o, :], const("ident"))
            mm.then_inc(s5_turn, 1)
            for j in range(4, 8):
                gemm("u", j, zx(zhi), zx(zlo), T2)
            pe.wait_ge(s5_bb, 1)

            def turn_xe(b):
                pe.wait_ge(xe_re, b + 1)
                pe.wait_ge(xe_done, b + 1)
                if b:
                    pe.wait_ge(we_done, b)
                for q in range(BP):
                    for c in range(2):
                        k = 2 * q + c
                        mm = pe.transpose(ps[:, 6 + k // 4, (k % 4) * P:(k % 4 + 1) * P], XE[b % 2][:, q, c, :],
                                          const("ident"))
                mm.then_inc(xe_t, 1)

            turn_xe(0)
            for b in range(NB5):
                if b + 1 < NB5:
                    turn_xe(b + 1)
                if b == 0:
                    pe.wait_ge(u5_in, 16 * KD * LC)
                else:
                    pe.wait_ge(e_done, b)
                pe.wait_ge(we_done, b + 1)
                for q in range(BP):
                    for r in range(2):
                        for c in range(2):
                            col0 = ((q % 2) * 2 + c) * NC5
                            mm = pe.matmul(ps[r * SP:(r + 1) * SP, 4 + q // 2, col0:col0 + NC5],
                                           WE[b % 2][:, q, c, r * SP:(r + 1) * SP], U5[:, 2 * (BP * b + q) + r, :],
                                           start=True, stop=True)
                mm.then_inc(e_mm, 1)

            def kernels(b):
                pe.wait_ge(wc_re, b + 1)
                pe.wait_ge(wc_done, b + 1)
                if b:
                    pe.wait_ge(k_out, b)
                for q in range(BP):
                    for c in range(2):
                        for g in range(2):
                            r = slice(SP * g, SP * g + SP)
                            mm = pe.matmul(ps[0:SH, 6 + g, q * P:(q + 1) * P], BB[r, c, BP * b + q, :],
                                           WC[b % 2][r, q, c, 0:P], start=c == 0, stop=c == 1)
                mm.then_inc(k_mm, 1)

            def outputs(b):
                pe.wait_ge(tt_in[b % 2], 16 * LC * (b // 2 + 1))
                pe.wait_ge(scan_done, SCAN_STEPS + 1)
                if b:
                    pe.wait_ge(y_done, b)
                else:
                    pe.wait_ge(e_done, NB5)
                for q in range(BP):
                    o = [ps[:, 4 + g, q * NC5:(q + 1) * NC5] for g in range(2)]
                    for g in range(2):
                        pe.matmul(o[g], TT[b % 2][:, 2 * q + g, :], U5[:, 8 * b + 2 * q + g, :], start=True, stop=False)
                    for c in range(2):
                        for g in range(2):
                            r = slice(SP * g, SP * g + SP)
                            mm = pe.matmul(o[g], WC[b % 2][r, q, c, SH:], S5[r, BP * b + q, c, 0:NC5],
                                           start=False, stop=c == 1)
                mm.then_inc(y_mm, 1)

            kernels(0)
            with pe.Fori(0, 2) as i:
                for j in range(4):
                    gemm("q", j, zx(zhi), zx(zlo), T2, i=i)
            for b in range(NB5):
                if b + 1 < NB5:
                    kernels(b + 1)
                outputs(b)
            with pe.Fori(0, 2) as i:
                for j in range(4):
                    gemm("glu", j, zx(yhi), zx(ylo), T2, i=i, fresh=(ylo_done, 0) if j == 0 else None)
            with pe.Fori(0, 2) as i:
                for j in range(4):
                    gemm("f", j, zx(zhi), zx(zlo), T2, i=i)
            for half in range(2):
                tokens_out("i%d" % half, 4, TB2, zx(zhi), zx(zlo), KD, 2)

            def before_states(h):
                pe.wait_ge(kin_done, h + 1)
                if h:
                    pe.wait_ge(sT_done, h)
                for b, t0 in enumerate(TS2):
                    w, q0 = (P, t0) if b < 4 else (CK, T2 - CK)
                    mm = pe.matmul(ps[:, 4 if b < 4 else 3, (b % 4) * P:(b % 4) * P + w], KH[:, h, t0:t0 + P],
                                   QH[:, h, q0:q0 + w], start=True, stop=True)
                mm.then_inc(gsc_mm, 1)
                pe.wait_ge(kout_done, h + 1)
                if h:
                    pe.wait_ge(ko_done, h)
                for b in range(4):
                    mm = pe.transpose(ps[:, 5, b * P:(b + 1) * P], kout[:, b * P:(b + 1) * P], const("ident"))
                mm.then_inc(kt_mm, 1)
                pe.wait_ge(q32_done, h + 1)
                for b in range(4):
                    mm = pe.matmul(ps[:, 3, 256 + 64 * b:320 + 64 * b].rearrange("p (k t) -> p k t", t=CK),
                                   KH[:, h, b * P:(b + 1) * P], second(QH[:, h, b * P:(b + 1) * P]),
                                   start=True, stop=True)
                mm.then_inc(gsc2_mm, 1)

            pe.wait_ge(rmask_done, 1)
            wait_job_out(pe, J["i1"] + 3)
            wait_job_out(pe, J["i1"] + 4)
            before_states(0)
            for h in range(HEADS):
                pe.wait_ge(ko_done, h + 1)
                for c in range(NB32):
                    n = NB32 * h + c
                    if n >= 3:
                        pe.wait_ge(st_done, n - 2)
                    r = slice(2 * CK * (c % 4), 2 * CK * (c % 4) + 2 * CK)
                    pe.matmul(ps[:, n % 3, 0:P], ko[r, c // 4, :], Vt[r, c // 4, h * P:(h + 1) * P],
                              start=True, stop=True).then_inc(dl_mm, 1)
                if h + 1 < HEADS:
                    before_states(h + 1)
                pe.wait_ge(sT_done, h + 1)
                if h:
                    pe.wait_ge(o_done, h)

                def o_cols(t0, w):
                    return ps[:, 6, t0:t0 + w] if t0 < 256 else ps[:, 7, t0 - 256:t0 - 256 + w]

                for b in range(TB2):
                    w, q0 = (P, TS2[b]) if b < 4 else (CK, T2 - CK)
                    pe.matmul(o_cols(q0, w), Vt[:, b, h * P:(h + 1) * P], sT[:, b, 0:w], start=True, stop=False,
                              skip_group_check=True)
                    for c in range(max(q0 // (2 * CK), 1), -(-(q0 + w) // (2 * CK))):
                        pe.wait_ge(st_done, NB32 * h + c)
                        n = min(2 * CK, T2 - 2 * CK * c)
                        mm = pe.matmul(o_cols(2 * CK * c, n), Sg[:, c - 1, :], QH[:, h, 2 * CK * c:2 * CK * c + n],
                                       start=False, stop=True, skip_group_check=True)
                mm.then_inc(o_mm, 1)
            for j in range(4):
                gemm("og", j, zx(zhi), zx(zlo), T2)
            for h in range(HEADS):
                pe.wait_ge(osq_done, h + 1)
                if h >= 2:
                    pe.wait_ge(oln_done, h - 1)
                for b, t0, t1 in halves(T2):
                    mm = pe.matmul(ps[:, 4 + 2 * (h % 2) + b, 0:HT2], const("ones"), KH[:, h, t0:t1], start=True, stop=True)
                mm.then_inc(ostat_mm, 1)
            for j in range(4, 8):
                gemm("og", j, zx(zhi), zx(zlo), T2)
            branches = ((zhi, zlo), (yahi, yalo), (zhi, zlo), (ybhi, yblo))
            for j, (hi, lo) in enumerate(branches):
                gemm("mrg", j, zx(hi), zx(lo), T2, fresh=(None, (yalo_done, 0), None, (yblo_done, 0))[j])
            with pe.Fori(0, KD - 1) as i:
                for j, (hi, lo) in enumerate(branches):
                    gemm("mrg", j + 4, zx(hi), zx(lo), T2, i=i)
            with pe.Fori(0, 2) as i:
                for j in range(4):
                    gemm("out", j, zx(zhi), zx(zlo), T2, i=i, fresh=(mrglo_done, 0) if j == 0 else None)
            norm_stats(5)
            ffn(1)
            norm_stats(6)
            pe.wait_ge(fin_done, KD)
            for t in range(QB):
                for half in range(2):
                    n = 2 * t + half
                    if n >= 2:
                        pe.wait_ge(ot_done, n - 1)
                    for k in range(4):
                        mm = pe.transpose(ps[:, 6 + n % 2, k * P:(k + 1) * P],
                                          xT[:, 4 * half + k, META + t * P:META + (t + 1) * P], const("ident"))
                    mm.then_inc(ot_mm, 1)

        @block.vector
        def _(dve):
            link = Chain(dve, v_link)

            def split_lo(u, i=None, step=4):
                dve.wait_ge(hi_done, plus(u + 1, i, step))
                dve.tensor_tensor(wlo[u % NHL][:], stage[plan.w_load[u] % NST][:], whi[u % NHL][:].bitcast(F32),
                                  ALU.subtract).then_inc(split_done, 1)

            def norm(n, units={}):
                s = NORMS[n]
                K, T, b = s["K"], s["T"], nbase[n]
                dve.wait_ge(rs_done, n + 1)

                def low(k):
                    dve.wait_ge(zhi_done, b + k + 1)
                    dve.scalar_tensor_tensor(out=s["lo"](k), in0=zu[:, (b + k) % NZU, 0:T],
                                             scalar=s["shift"](k) if s["shift"] else 0.0,
                                             in1=s["hi"](k).bitcast(F32), op0=ALU.add, op1=ALU.subtract)\
                       .then_inc(zlo_done, 1)

                for k in range(K):
                    if b + k >= NZU:
                        dve.wait_ge(zlo_done, b + k - NZU + 1)
                    dve.scalar_tensor_tensor(out=zu[:, (b + k) % NZU, 0:T], in0=s["src"](k), scalar=s["gain"](k),
                                             in1=rs[:, 0:T], op0=ALU.mult, op1=ALU.mult).then_inc(zu_done, 1)
                    if k:
                        low(k - 1)
                    if k - 1 in units:
                        split_lo(units[k - 1])
                low(K - 1)

            for counter in (conv_done, glo_done, scan_done, ya_done, og_done, mrg_done):
                dve.sem_inc(counter, 1)
            dve.wait_ge(prow_t, 1)
            dve.tensor_copy(par[:, 0:NROWS], ps[:, 4, 0:NROWS]).then_inc(par_done, 1)
            dve.wait_ge(meta_t, 1)
            dve.tensor_copy(xT[:, :, 0:META], ps[:, 7, 0:KD * META].rearrange("p (k t) -> p k t", k=KD))\
               .then_inc(meta_done, 1)
            def ada(a):
                g, k = divmod(a, KD)
                if a < PRE:
                    w = early[a]
                    dve.wait_ge(early_in[a], 16)
                else:
                    slot, value = plan.landed[plan.ada_load[a - PRE]]
                    w = stage[slot]
                    dve.wait_ge(landed[slot], value)
                if k == 0:
                    if g >= 2:
                        dve.wait_ge(mod_mm, g - 1)
                    dve.tensor_scalar(asum[g % 2][:, :], w[:, :], csil[:, k:k + 1], None, ALU.mult)\
                       .then_inc(ada_done, 1)
                else:
                    dve.wait_ge(ada_done, a)
                    dve.scalar_tensor_tensor(out=asum[g % 2][:, :], in0=w[:, :], scalar=csil[:, k:k + 1],
                                             in1=asum[g % 2][:, :], op0=ALU.mult, op1=ALU.add).then_inc(ada_done, 1)

            link(dve.tensor_copy(posf[:, :], posi[:, :]))
            misc = cst[:, CONST["misc"]:CONST["misc"] + P]

            def table(w):
                a, r, t = tab[:, 2 * w, :], angt[:, 0, :], angt[:, 1, :]
                link(dve.tensor_scalar(r, posf[:, :], misc[:, w:w + 1], None, ALU.mult))
                link(dve.tensor_scalar(t, r, 1.0 / (2 * np.pi), MAGIC, ALU.mult, ALU.add))
                link(dve.tensor_scalar(t, t, MAGIC, None, ALU.subtract))
                link(dve.scalar_tensor_tensor(out=r, in0=t, scalar=-TWO_PI_HI, in1=r, op0=ALU.mult, op1=ALU.add))
                link(dve.scalar_tensor_tensor(out=r, in0=t, scalar=-TWO_PI_LO, in1=r, op0=ALU.mult, op1=ALU.add))
                link(dve.tensor_scalar(tab[:, 2 * w + 1, :], r, PI, -PI, ALU.min, ALU.max))
                link(dve.tensor_scalar(t, r, np.pi / 2, -2 * np.pi, ALU.is_gt, ALU.mult))
                link(dve.scalar_tensor_tensor(out=a, in0=r, scalar=np.pi / 2, in1=t, op0=ALU.add, op1=ALU.add))
                dve.tensor_scalar(a, a, PI, -PI, ALU.min, ALU.max).then_inc(tab_ready, 1)

            dve.wait_ge(s_silu, 1)
            for a in range(16):
                ada(a)
            dve.wait_ge(mod_mm, 2)
            link(dve.tensor_tensor(mod[:, 0:16], ps[:, 7, 128:144], par[:, ROW["b_ada"]:ROW["b_ada"] + 16], ALU.add))
            link(dve.scalar_tensor_tensor(out=gsc[:, 0, :], in0=mod[:, 8:16], scalar=1.0,
                                          in1=par[:, ROW["g_mix"]:ROW["g_mix"] + 8], op0=ALU.add, op1=ALU.mult))
            norm(0, {2: 0, 4: 1, 6: 2})
            for u in range(3, U["kpe"] + 3):
                split_lo(u)
                if u in (4, 6):
                    table(u // 2 - 2)
            norm(1)
            norm(2)
            for u in range(U["kpe"] + 3, U["dv"] + 3 + 4):
                split_lo(u)

            def group_mul(g):
                s = GROUPS[g]
                dve.wait_ge(grs_done, g + 1)
                for m, t in enumerate(s["tiles"]):
                    ins = dve.scalar_tensor_tensor(out=HT[:, t, :], in0=HT[:, t, :], scalar=col(s["gain"][m]),
                                                   in1=sqg[g % 2][:, m, :], op0=ALU.mult, op1=ALU.mult)
                ins.then_inc(gq_done if s["rot"] else ghead_done, 1)

            def group_rot(g):
                s = GROUPS[g]
                n, t0, w = len(s["tiles"]), s["tiles"][0], 0 if s["w"] == 64 else 2
                dve.wait_ge(grot_mm, ROTS.index(g) + 1)
                dve.wait_ge(tab_done, 1)
                if g:
                    dve.wait_ge(ghead_done, g)
                dve.tensor_tensor(rt[g % 2][:, 0:n, :], ps[:, 4:4 + n, :],
                                  tab[:, w + 1:w + 2, :].to_broadcast([P, n, T1]), ALU.mult).then_inc(gsin_done, 1)
                dve.wait_ge(gsin_done, ROTS.index(g) + 1)
                dve.wait_ge(gcos_done, ROTS.index(g) + 1)
                dve.tensor_tensor(HT[:, t0:t0 + n, :], HT[:, t0:t0 + n, :], rt[g % 2][:, 0:n, :], ALU.add)\
                   .then_inc(ghead_done, 1)

            group_mul(0)
            split_lo(U["kn"])
            split_lo(U["mv"])
            group_rot(0)
            group_mul(1)
            group_rot(1)
            group_mul(2)
            group_mul(3)
            group_mul(4)
            group_rot(4)

            def masked(q):
                kind, h, i = STEPS[q]
                w, b = (i + 1) * P, q % 4
                scale = (HD + RD if kind == "mla" else HD) ** -0.5
                dve.wait_ge(at_s, q + 1)
                if q >= 4:
                    dve.wait_ge(at_t, q - 3)
                dve.tensor_tensor_reduce(pb[:, b, 0:w], ps[:, q % 2, 0:w],
                                         cst[:, CONST[kind] + 512 - w:CONST[kind] + 512], scale, -3e38, ALU.add,
                                         ALU.max, small[:, 16 + b:17 + b]).then_inc(at_mask, 1)
                dve.wait_ge(at_mask, q + 1)
                dve.tensor_scalar(small[:, 8 + b:9 + b], small[:, 16 + b:17 + b], -1.0, None, ALU.mult).then_inc(at_neg, 1)

            def normed(q):
                w, b = (STEPS[q][2] + 1) * P, q % 4
                dve.wait_ge(at_exp, q + 1)
                link(dve.reciprocal(small[:, 20 + b:21 + b], small[:, 12 + b:13 + b]))
                dve.tensor_scalar(pb[:, b, 0:w], pb[:, b, 0:w], small[:, 20 + b:21 + b], None, ALU.mult).then_inc(at_p, 1)

            for t in range(NS + 4):
                if t < NS:
                    masked(t)
                if 1 <= t <= NS:
                    normed(t - 1)
                if t < NS and t % 2 == 0:
                    ada(16 + t // 2)
                if t >= 4 and (t - 4) % 8 == 7:
                    m = (t - 4) // 8
                    dve.wait_ge(mixhi, m + 1)
                    dve.tensor_tensor(mlo[:, m, :], ps[:, 4 + m % 2, :], mhi[:, m, :].bitcast(F32), ALU.subtract)\
                       .then_inc(mixlo, 1)
            dve.wait_ge(mod_mm, 6)
            link(dve.tensor_tensor(mod[:, 16:48], ps[:, 7, 144:176], par[:, ROW["b_ada"] + 16:ROW["b_ada"] + 48], ALU.add))
            link(dve.scalar_tensor_tensor(out=gsc[:, 1, :], in0=mod[:, 32:40], scalar=1.0,
                                          in1=par[:, ROW["g_ffn"]:ROW["g_ffn"] + 8], op0=ALU.add, op1=ALU.mult))
            for u in range(3):
                split_lo(U["wo"] + u)

            def residual(job, T, gate, m, i, base):
                dve.wait_ge(marks, plus(plan.full[job], i, 4))
                x = xT[:, bass.ds(plus(m, i, 4), 1), META if T == T1 else 0:T2]
                x = wide(x.rearrange("p a t -> p (a t)"), T)
                if gate is not None:
                    ins = dve.scalar_tensor_tensor(out=x, in0=acc(job, T), scalar=mod[:, bass.ds(plus(gate + m, i, 4), 1)],
                                                   in1=x, op0=ALU.mult, op1=ALU.add)
                else:
                    ins = dve.tensor_tensor(x, acc(job, T), x, ALU.add)
                ins.then_inc(emptied[job % 2], 1)

            with dve.Fori(0, 2) as i:
                for j in range(4):
                    split_lo(U["wo"] + 3 + j, i)
                    residual(J["wo"] + j, T1, 16, j, i, 0)
            wait_residual(dve, "wo", 8)
            norm(3)

            def ffn(b):
                f = FFNS[b]
                T, key = f["T"], f["key"]
                link(dve.memset(ub[:, :, 0:2], 0.0))
                for kind, c, n in FFN_ORDER:
                    job0, u0 = J[key + kind + str(c)], U[key + kind + str(c)]
                    pair0 = 22 * b + 8 * c
                    last = b == len(FFNS) - 1 and (kind, c) == ("down", 2)
                    if kind == "down" and c:
                        wait_residual(dve, key + "down" + str(c - 1), 8)
                    with dve.Fori(0, n // 4 - (1 if last else 0)) as i:
                        link.loop(i, 6 if kind == "up" else 0)
                        for j in range(4):
                            split_lo(u0 + 3 + j, i)
                            if kind == "down":
                                residual(job0 + j, T, f["g2"], j, i, 0)
                            else:
                                conv(f, c, job0, pair0, i, j)
                    link.end(n // 4 - (1 if last else 0))
                    if last:
                        split_lo(u0 + n - 1)
                        for j in range(n - 4, n):
                            residual(job0 + j, T, f["g2"], j, None, 0)

            def conv(f, c, job0, pair0, i, j):
                T, q, g = f["T"], j // 2, j % 2
                ft = 8 * c + q + (NF if g else 0)
                job = job0 + j

                def tap(k):
                    o = ROW[f["cw"]] + 2 * NF * k + ft
                    return par[:, bass.ds(i * 2 + o, 1)]

                o = cv[:, q, g, 0:T]
                wait_job_out(dve, job, i)
                if not g:
                    dve.wait_ge(glo_done, plus(max(pair0 + q - 1, 0) + 1, i, 2))
                link(dve.tensor_scalar(o, ub[:, g, 2:2 + T], tap(2), par[:, bass.ds(i * 2 + (ROW[f["cb"]] + ft), 1)],
                                       ALU.mult, ALU.add))
                if g == 0:
                    link(dve.scalar_tensor_tensor(out=o, in0=ub[:, g, 1:1 + T], scalar=tap(1), in1=o,
                                                  op0=ALU.mult, op1=ALU.add))
                else:
                    dve.scalar_tensor_tensor(out=o, in0=ub[:, g, 1:1 + T], scalar=tap(1), in1=o,
                                             op0=ALU.mult, op1=ALU.add).then_inc(conv_mid, 1)
                    dve.wait_ge(conv_mid, i * 2 + (pair0 + q + 1))
                dve.scalar_tensor_tensor(out=o, in0=ub[:, g, 0:T], scalar=tap(0), in1=o,
                                         op0=ALU.mult, op1=ALU.add).then_inc(conv_done, 1)
                if g:
                    k = bass.ds(i * 2 + q, 1)
                    dve.wait_ge(silu_done, i * 2 + (pair0 + q + 1))
                    dve.wait_ge(conv_done, i * 4 + (2 * pair0 + j + 2))
                    dve.tensor_tensor(o, cv[:, q, 0, 0:T], o, ALU.mult).then_inc(gf_done, 1)
                    dve.wait_ge(ghi_done, i * 2 + (pair0 + q + 1))
                    dve.tensor_tensor(glo[c % 2][:, k, 0:T].rearrange("p a t -> p (a t)"), o,
                                      ghi[c % 2][:, k, 0:T].rearrange("p a t -> p (a t)").bitcast(F32),
                                      ALU.subtract).then_inc(glo_done, 1)

            ffn(0)

            wait_residual(dve, "b1down2", 8)
            norm(4)
            for j in range(4):
                split_lo(U["u"] + 3 + j)
            dve.wait_ge(s5_in, 16 * 22)
            dve.tensor_copy(s5row[:, 2, :].rearrange("q (r p) -> q r p", r=2),
                            dtrow[:, :].unsqueeze(2).to_broadcast([PAIRS, 2, SP])).then_inc(dt_wide, 1)
            dve.wait_ge(s5_turn, 1)
            dve.tensor_copy(CC[:, 0, :, :], ps[:, 7, :].rearrange("p (q h) -> p q h", h=SH))
            dve.tensor_copy(CC[:, 1, :, :], ps[:, 4, :].rearrange("p (q h) -> p q h", h=SH))
            dve.tensor_copy(Dg[:, :], ps[0:SH, 6, 3 * PAIRS:3 * PAIRS + SG])
            dve.tensor_copy(v5[:, 0:3, :], ps[:, 6, 0:3 * PAIRS].rearrange("p (c q) -> p c q", c=3)).then_inc(s5_vec, 1)
            dve.tensor_tensor(gsc[:, 2, :], par[:, ROW["lb"]:ROW["lb"] + 8], par[:, ROW["lb"] + 8:ROW["lb"] + 16],
                              ALU.subtract).then_inc(lb_in, 1)
            lr, li, dt, mag, th, turns, t6, sin, cos, ab_re, ab_im, nr, den, co_re, co_im, t15 = (
                v5[:, k, :] for k in range(16))
            dve.wait_ge(s5_exp, 1)
            dve.tensor_tensor(mag, lr, dt, ALU.mult).then_inc(s5_vec, 1)
            link(dve.tensor_tensor(th, li, dt, ALU.mult))
            link(dve.tensor_scalar(turns, th, 1.0 / (2 * np.pi), MAGIC, ALU.mult, ALU.add))
            link(dve.tensor_scalar(turns, turns, MAGIC, None, ALU.subtract))
            link(dve.scalar_tensor_tensor(out=th, in0=turns, scalar=-TWO_PI_HI, in1=th, op0=ALU.mult, op1=ALU.add))
            link(dve.scalar_tensor_tensor(out=th, in0=turns, scalar=-TWO_PI_LO, in1=th, op0=ALU.mult, op1=ALU.add))
            link(dve.tensor_scalar(sin, th, PI, -PI, ALU.min, ALU.max))
            link(dve.tensor_scalar(turns, th, np.pi / 2, -2 * np.pi, ALU.is_gt, ALU.mult))
            link(dve.scalar_tensor_tensor(out=cos, in0=th, scalar=np.pi / 2, in1=turns, op0=ALU.add, op1=ALU.add))
            dve.tensor_scalar(cos, cos, PI, -PI, ALU.min, ALU.max).then_inc(s5_vec, 1)
            dve.wait_ge(lb_sig, 1)
            link(dve.tensor_scalar(gsc[:, 3, :], gsc[:, 2, :], -1.0, 1.0, ALU.mult, ALU.add))
            dve.tensor_scalar(gsc[:, 0, :], gsc[:, 3, :], -1.0, None, ALU.mult).then_inc(lb_done, 1)

            def product(o_re, o_im, a_re, a_im, b_re, b_im, ta, tb):
                link(dve.tensor_tensor(ta, a_re, b_re, ALU.mult))
                link(dve.tensor_tensor(tb, a_im, b_im, ALU.mult))
                link(dve.tensor_tensor(o_re, ta, tb, ALU.subtract))
                link(dve.tensor_tensor(ta, a_re, b_im, ALU.mult))
                link(dve.tensor_tensor(tb, a_im, b_re, ALU.mult))
                link(dve.tensor_tensor(o_im, ta, tb, ALU.add))

            def over_h(v):
                return v.unsqueeze(2).to_broadcast([P, PAIRS, SH])

            def temp(t, n, *shape):
                v = t[:, :, :].rearrange("p a b -> p (a b)")[:, 0:n]
                return v.rearrange("p (a b) -> p a b", a=shape[0])

            def double(n):
                by = [Pw[:, c, n:n + 1, :].to_broadcast([P, n, PAIRS]) for c in range(2)]
                product(Pw[:, 0, n + 1:2 * n + 1, :], Pw[:, 1, n + 1:2 * n + 1, :], Pw[:, 0, 1:n + 1, :],
                        Pw[:, 1, 1:n + 1, :], by[0], by[1], temp(tw, n * PAIRS, n), temp(tv, n * PAIRS, n))
            split_lo(U["u"] + 7)
            dve.wait_ge(s5_exp, 2)
            dve.wait_ge(s5_sin, 1)
            link(dve.tensor_tensor(ab_re, mag, cos, ALU.mult))
            link(dve.tensor_tensor(ab_im, mag, sin, ALU.mult))
            link(dve.tensor_scalar(nr, ab_re, 1.0, None, ALU.subtract))
            link(dve.tensor_tensor(den, lr, lr, ALU.mult))
            link(dve.tensor_tensor(t6, li, li, ALU.mult))
            link(dve.tensor_tensor(den, den, t6, ALU.add))
            link(dve.reciprocal(den, den))
            link(dve.tensor_tensor(co_re, nr, lr, ALU.mult))
            link(dve.tensor_tensor(t6, ab_im, li, ALU.mult))
            link(dve.tensor_tensor(co_re, co_re, t6, ALU.add))
            link(dve.tensor_tensor(co_re, co_re, den, ALU.mult))
            link(dve.tensor_tensor(co_im, ab_im, lr, ALU.mult))
            link(dve.tensor_tensor(t6, nr, li, ALU.mult))
            link(dve.tensor_tensor(co_im, co_im, t6, ALU.subtract))
            link(dve.tensor_tensor(co_im, co_im, den, ALU.mult))

            split_lo(U["u"] + 8)
            product(BB[:, 0, :, :], BB[:, 1, :, :], over_h(co_re), over_h(co_im), braw[:, 0, :, :], braw[:, 1, :, :],
                    temp(tw, PAIRS * SH, PAIRS), temp(tv, PAIRS * SH, PAIRS))
            split_lo(U["u"] + 9)
            link(dve.memset(Pw[:, 0, 0, :], 1.0))
            link(dve.memset(Pw[:, 1, 0, :], 0.0))
            link(dve.tensor_copy(Pw[:, 0, 1, :], ab_re))
            link(dve.tensor_copy(Pw[:, 1, 1, :], ab_im))
            double(1)
            double(2)
            split_lo(U["u"] + 10)
            double(4)
            for j in range(LC):
                link(dve.tensor_copy(Pr[:, :, j, :], Pw[:, :, LC - 1 - j, :]))
            link(dve.tensor_scalar(Pw[:, 1, :, :], Pw[:, 1, :, :], -1.0, None, ALU.mult))
            link(dve.tensor_copy(AA[:, :, 0, 0], Pw[:, 0, LC, :]))
            link(dve.tensor_copy(AA[:, :, 0, 1], Pw[:, 1, LC, :]))
            link(dve.tensor_scalar(AA[:, :, 1, 0], Pw[:, 1, LC, :], -1.0, None, ALU.mult))
            link(dve.tensor_copy(AA[:, :, 1, 1], Pw[:, 0, LC, :]))
            dve.memset(S5[:, :, :, 0:1], 0.0).then_inc(s5_bb, 1)

            def xe_real(b):
                q = slice(BP * b, BP * b + BP)
                if b >= 2:
                    dve.wait_ge(xe_t, b - 1)
                shape = [P, BP, LC, SH]
                o = XE[b % 2][:, :, 0, :].rearrange("p q (j h) -> p q j h", h=SH)
                t = tw[:, :, 0:P].rearrange("p q (j h) -> p q j h", h=SH)
                pw = [Pr[:, c, :, q].rearrange("p j q -> p q j").unsqueeze(3).to_broadcast(shape) for c in range(2)]
                bb = [BB[:, c, q, :].unsqueeze(2).to_broadcast(shape) for c in range(2)]
                link(dve.tensor_tensor(o, pw[0], bb[0], ALU.mult))
                link(dve.tensor_tensor(t, pw[1], bb[1], ALU.mult))
                dve.tensor_tensor(o, o, t, ALU.subtract).then_inc(xe_re, 1)
                dve.wait_ge(xe_re, b + 1)

            xe_real(0)
            for b in range(NB5):
                if b + 1 < NB5:
                    xe_real(b + 1)
                dve.wait_ge(e_mm, b + 1)
                dve.tensor_copy(S5[:, BP * b:BP * b + BP, :, 1:NC5 + 1].rearrange("p (b q) c t -> p b (q c) t", b=2),
                                ps[:, 4:6, 0:4 * NC5].rearrange("p b (k t) -> p b k t", k=4)).then_inc(e_done, 1)

            def wc_real(b):
                q = slice(BP * b, BP * b + BP)
                if b >= 2:
                    dve.wait_ge(y_mm, b - 1)
                else:
                    dve.wait_ge(xe_t, NB5)
                shape = [P, BP, LC + 1, SH]
                o = WC[b % 2][:, :, 0, :].rearrange("p q (j h) -> p q j h", h=SH)
                t = tw[:, :, :].rearrange("p q (j h) -> p q j h", h=SH)
                pw = [Pw[:, c, :, q].rearrange("p j q -> p q j").unsqueeze(3).to_broadcast(shape) for c in range(2)]
                cc = [CC[:, c, q, :].unsqueeze(2).to_broadcast(shape) for c in range(2)]
                link(dve.tensor_tensor(o, pw[0], cc[0], ALU.mult))
                link(dve.tensor_tensor(t, pw[1], cc[1], ALU.mult))
                dve.tensor_tensor(o, o, t, ALU.add).then_inc(wc_re, 1)
                dve.wait_ge(wc_re, b + 1)

            def skip(b):
                shape = [SH, 2 * BP, SH]
                link(dve.tensor_tensor(dtmp[:, :, :], const("ident", SH, SH).unsqueeze(1).to_broadcast(shape),
                                       Dg[:, 8 * b:8 * b + 8].unsqueeze(2).to_broadcast(shape), ALU.mult))
                dve.wait_ge(k_out, b + 1)
                dve.tensor_tensor(K16[b % 2][:, :, 0:SH], K16[b % 2][:, :, 0:SH], dtmp[:, :, :], ALU.add)\
                   .then_inc(k_done, 1)
                dve.wait_ge(k_done, b + 1)

            wc_real(0)
            skip(0)
            wc_real(1)
            dve.wait_ge(e_done, NB5)
            with dve.Fori(0, 2) as i:
                for j in range(SCAN_STEPS // 2):
                    if j % 8 == 0:
                        split_lo(U["q"] + 3 + j // 8, i)
                    c, c1 = (bass.ds(i * (SCAN_STEPS // 2) + (j + k), 1) for k in (1, 2))
                    dve.wait_ge(scan_done, plus(j + 1, i, SCAN_STEPS // 2))
                    dve.tensor_tensor(sc5[:, :, :, :], AA[:, :, :, :],
                                      S5[:, :, :, c].rearrange("p q c a -> p q (a c)").unsqueeze(2)
                                      .to_broadcast([P, PAIRS, 2, 2]), ALU.mult).then_inc(scan_t, 1)
                    dve.wait_ge(scan_t, plus(j + 1, i, SCAN_STEPS // 2))
                    nxt = S5[:, :, :, c1].rearrange("p q c a -> p q (a c)")
                    dve.tensor_tensor(nxt, nxt, sc5[:, :, :, 0], ALU.add).then_inc(scan_u, 1)
                    dve.wait_ge(scan_u, plus(j + 1, i, SCAN_STEPS // 2))
                    dve.tensor_tensor(nxt, nxt, sc5[:, :, :, 1], ALU.add).then_inc(scan_done, 1)
            skip(1)
            for b in range(2, NB5):
                wc_real(b)
                skip(b)
            for k in range(KD):
                dve.wait_ge(yhi_done, k + 1)
                dve.tensor_tensor(ylo[:, k, :], y5[:, k, :], yhi[:, k, :].bitcast(F32), ALU.subtract).then_inc(ylo_done, 1)

            def flat(ap, i, j):
                return ap[:, bass.ds(plus(j, i, 4), 1), :].rearrange("p a t -> p (a t)")

            with dve.Fori(0, 2) as i:
                for j in range(4):
                    split_lo(U["glu"] + 3 + j, i)
                    wait_job_out(dve, J["glu"] + j, i)
                    dve.tensor_tensor(flat(y5, i, j), flat(y5, i, j), gat[:, j % 2, :], ALU.mult).then_inc(ya_done, 1)
            with dve.Fori(0, 2) as i:
                for j in range(4):
                    split_lo(U["f"] + 3 + j, i)
            split_lo(U["i0"] + 3)
            dve.wait_ge(rmask_done, 1)
            wait_residual(dve, "q", 8)

            def into_gates(h):
                dve.wait_ge(ep_done, h + 1)
                link(dve.tensor_tensor(QH[:, h, :], QH[:, h, :], ex[:, h % 2, :], ALU.mult))
                link(dve.tensor_copy(dec[:, h, :], ex[:, h % 2, :].rearrange("p (c t) -> p c t", t=CK)[:, :, CK - 1]))
                pairs = dec[:, h, 0:NCK - 1].rearrange("p (c r) -> p c r", r=2)
                dve.tensor_tensor(dec2[:, h, :], pairs[:, :, 0], pairs[:, :, 1], ALU.mult).then_inc(dec_done, 1)
                dve.wait_ge(em_done, h + 1)
                dve.wait_ge(cum_done, h + 1)
                dve.tensor_tensor(KH[:, h, :], KH[:, h, :], LF[:, h, :], ALU.mult).then_inc(kin_done, 1)

            for h in range(HEADS):
                dve.wait_ge(lf_done, h + 1)
                link(dve.tensor_tensor_scan(LF[:, h, :], rmask[:, :], LF[:, h, :], 0.0, ALU.mult, ALU.add))
                dve.tensor_scalar(KH[:, h, :], KH[:, h, :], gsc[:, 0, h:h + 1], gsc[:, 3, h:h + 1], ALU.mult, ALU.add)\
                   .then_inc(cum_done, 1)
            for h in range(4):
                into_gates(h)
            for u in range(4):
                split_lo(U["i1"] + u)
            for h in range(4, HEADS):
                into_gates(h)
            for u in range(3):
                split_lo(U["og"] + u)
            dve.wait_ge(kin_done, HEADS)
            for h in range(HEADS):
                dve.wait_ge(gsc_mm, h + 1)
                if h:
                    dve.wait_ge(o_mm, h)
                mask = const("chunk")
                link(dve.copy_predicated(sT[:, 0:4, :], mask.bitcast(I32).unsqueeze(1).to_broadcast([P, 4, P]),
                                         ps[:, 4, :].rearrange("p (b t) -> p b t", b=4)))
                dve.wait_ge(gsc2_mm, h + 1)
                dve.copy_predicated(sT[:, 4, 0:CK], mask[:, P - CK:P].bitcast(I32), ps[:, 3, 0:CK])
                mask = cst[:, CONST["misc"] + 64:CONST["misc"] + P].bitcast(I32).rearrange("p (k t) -> p k t", t=CK)
                dve.copy_predicated(sT[:, 0:4, :].rearrange("p b (k r t) -> p b k r t", r=2, t=CK)[:, :, :, 1, :],
                                    mask.unsqueeze(1).to_broadcast([P, 4, 4, CK]),
                                    ps[:, 3, 256:512].rearrange("p (b k t) -> p b k t", b=4, t=CK)).then_inc(sT_done, 1)
                for c in range(NB32):
                    n = NB32 * h + c
                    dve.wait_ge(dl_mm, n + 1)
                    delta = ps[:, n % 3, 0:P]
                    if c == 0:
                        dve.tensor_copy(Sg[:, c, :], delta).then_inc(st_done, 1)
                    else:
                        dve.wait_ge(st_done, n)
                        dve.scalar_tensor_tensor(out=Sg[:, c, :], in0=Sg[:, c - 1, :], scalar=dec2[:, h, c:c + 1],
                                                 in1=delta, op0=ALU.mult, op1=ALU.add).then_inc(st_done, 1)
            for j in range(4):
                split_lo(U["og"] + 3 + j)
            for h in range(HEADS):
                dve.wait_ge(ors_done, h + 1)
                dve.scalar_tensor_tensor(out=QH[:, h, :], in0=QH[:, h, :], scalar=col("hg"), in1=KH[:, h, :],
                                         op0=ALU.mult, op1=ALU.mult).then_inc(on_done, 1)
            dve.wait_ge(on_done, HEADS)

            def gated(k):
                wait_job_out(dve, J["og"] + k)
                dve.tensor_tensor(QH[:, k, :], QH[:, k, :], og[:, k, :], ALU.mult).then_inc(og_done, 1)

            dve.wait_ge(ya_done, KD + 1)
            for j in range(4, 8):
                split_lo(U["og"] + 3 + j)
                for k in (2 * j - 8, 2 * j - 7):
                    dve.wait_ge(yahi_done, k + 1)
                    dve.tensor_tensor(yalo[:, k, :], y5[:, k, :], yahi[:, k, :].bitcast(F32), ALU.subtract)\
                       .then_inc(yalo_done, 1)
                gated(j - 4)
            for k in range(4, 8):
                gated(k)
            for k in range(KD):
                dve.wait_ge(ybhi_done, k + 1)
                dve.tensor_tensor(yblo[:, k, :], QH[:, k, :], ybhi[:, k, :].bitcast(F32), ALU.subtract)\
                   .then_inc(yblo_done, 1)
            dve.wait_ge(yblo_done, KD)
            with dve.Fori(0, 8) as i:
                for j in range(4):
                    split_lo(U["mrg"] + 3 + j, i)
                    if j % 2:
                        job = J["mrg"] + j
                        wait_job_out(dve, job - 1, i)
                        dve.wait_ge(marks, plus(plan.full[job], i, 4))
                        m, gate = mrg[:, bass.ds(i, 1), :].rearrange("p a t -> p (a t)"), gat[:, j // 2, :]
                        o = m if j == 1 else gate
                        dve.tensor_tensor(wide(o, T2), acc(job, T2), wide(gate, T2), ALU.mult)\
                           .then_inc(emptied[job % 2], 1)
                        if j == 3:
                            wait_job_out(dve, job, i)
                            dve.tensor_tensor(m, m, gate, ALU.add).then_inc(mrg_done, 1)
            dve.wait_ge(mrg_done, KD + 1)
            for k in range(KD):
                dve.wait_ge(mrghi_done, k + 1)
                dve.tensor_tensor(zlo[:, k, :], mrg[:, k, :], zhi[:, k, :].bitcast(F32), ALU.subtract)\
                   .then_inc(mrglo_done, 1)
            with dve.Fori(0, 2) as i:
                for j in range(4):
                    split_lo(U["out"] + 3 + j, i)
                    residual(J["out"] + j, T2, None, j, i, 0)
            wait_residual(dve, "out", 8)
            norm(5)
            ffn(1)
            wait_residual(dve, "b2down2", 8)
            dve.wait_ge(rs_done, 7)
            for k in range(KD):
                x = tok(xT, k, T1)
                dve.scalar_tensor_tensor(out=x, in0=x, scalar=NORMS[6]["gain"](k), in1=rs[:, 0:T1],
                                         op0=ALU.mult, op1=ALU.mult).then_inc(fin_done, 1)

        @block.gpsimd
        def _(pool):
            for name, src, rep in HEAD_PARAMS:
                b, p0 = divmod(ROW[name], P)
                w = P // rep
                for r in range(rep):
                    pool.dma_start(prow[p0:p0 + 1, b, r * w:(r + 1) * w], A[src][0:1, :]).then_inc(s_par2, 16)
            pool.dma_start(posi[:, :], A["positions"][0:1, :].to_broadcast([P, SEQ])).then_inc(s_par2, 16)
            pool.dma_start(metar[:, :], A["meta_tokens_2"]).then_inc(s_meta, 16)
            pool.memset(small[:, 0:8], EPS).then_inc(pads, 1)
            for n, g in enumerate(ROTS):
                s = GROUPS[g]
                m, t0, w = len(s["tiles"]), s["tiles"][0], 0 if s["w"] == 64 else 2
                pool.wait_ge(grot_mm, n + 1)
                pool.wait_ge(tab_done, 1)
                pool.tensor_tensor(HT[:, t0:t0 + m, :], HT[:, t0:t0 + m, :],
                                   tab[:, w:w + 1, :].to_broadcast([P, m, T1]), ALU.mult).then_inc(gcos_done, 1)
            plink = Chain(pool, p_link)
            pool.wait_ge(marks, plan.full[J["b1down2"] + 7])
            pool.wait_ge(glo_done, NF + 1)
            lam = lambda n: A[n][0].rearrange("(q r) p -> q (r p)", r=2)
            pool.dma_start(s5row[:, 0, :], lam("ssm_lambda_re_2")).then_inc(s5_in, 16)
            pool.dma_start(s5row[:, 1, :], lam("ssm_lambda_im_2")).then_inc(s5_in, 16)
            pool.dma_start(dtrow[:, :], A["ssm_log_dt_2"][0].rearrange("(q r) -> q r", r=2)).then_inc(s5_in, 16)
            for c, n in enumerate(("ssm_b_re_2", "ssm_b_im_2")):
                pool.dma_start(braw[:, c, :, :], A[n][0].rearrange("(q r) p h -> (r p) q h", r=2)).then_inc(s5_in, 16)
            for c, n in enumerate(("ssm_c_re_2", "ssm_c_im_2")):
                v = A[n][0].rearrange("(o q r) h p -> o r q h p", q=8, r=2)
                for o in range(4):
                    for r in range(2):
                        pool.dma_start(crow[:, c, o, r * SP:(r + 1) * SP], v[o, r]).then_inc(s5_in, 16)
            pool.dma_start(drow[:, :], A["ssm_d_2"][0].rearrange("(g h) -> g h", h=SH)).then_inc(s5_in, 16)
            pool.wait_ge(zlo_done, nbase[5])
            plink(pool.memset(rmask[:, :], 1.0))
            pool.memset(rmask[:, :].rearrange("p (c t) -> p c t", t=CK)[:, :, 0], 0.0)
            pool.memset(sT[:, :, :], 0.0).then_inc(rmask_done, 1)
            for k in range(KD):
                wait_job_out(pool, J["u"] + k)
                if k:
                    pool.wait_ge(us_out, 16 * k)
                pool.dma_start(u_dram[k], uD[:, k, :, :]).then_inc(us_out, 16)
            pool.wait_ge(s5_bb, 1)
            for b in range(NB5):
                q = slice(BP * b, BP * b + BP)
                if b >= 2:
                    pool.wait_ge(xe_t, b - 1)
                shape = [P, BP, LC, SH]
                o = XE[b % 2][:, :, 1, :].rearrange("p q (j h) -> p q j h", h=SH)
                t = tx[:, :, :].rearrange("p q (j h) -> p q j h", h=SH)
                pw = [Pr[:, c, :, q].rearrange("p j q -> p q j").unsqueeze(3).to_broadcast(shape) for c in range(2)]
                bb = [BB[:, c, q, :].unsqueeze(2).to_broadcast(shape) for c in range(2)]
                plink(pool.tensor_tensor(o, pw[0], bb[1], ALU.mult))
                plink(pool.tensor_tensor(t, pw[1], bb[0], ALU.mult))
                pool.tensor_tensor(o, o, t, ALU.add).then_inc(xe_done, 1)
                pool.wait_ge(xe_done, b + 1)

            for b in range(NB5):
                q = slice(BP * b, BP * b + BP)
                if b >= 2:
                    pool.wait_ge(y_mm, b - 1)
                else:
                    pool.wait_ge(xe_t, NB5)
                shape = [P, BP, LC + 1, SH]
                o = WC[b % 2][:, :, 1, :].rearrange("p q (j h) -> p q j h", h=SH)
                t = tv[:, :, :].rearrange("p q (j h) -> p q j h", h=SH)
                pw = [Pw[:, c, :, q].rearrange("p j q -> p q j").unsqueeze(3).to_broadcast(shape) for c in range(2)]
                cc = [CC[:, c, q, :].unsqueeze(2).to_broadcast(shape) for c in range(2)]
                plink(pool.tensor_tensor(o, pw[1], cc[0], ALU.mult))
                plink(pool.tensor_tensor(t, pw[0], cc[1], ALU.mult))
                pool.tensor_tensor(o, o, t, ALU.subtract).then_inc(wc_done, 1)
                pool.wait_ge(wc_done, b + 1)
                if b == 0:
                    pool.wait_ge(e_mm, NB5)
                    for k in range(2):
                        ins = pool.memset(TT[k][:, :, :], 0.0)
                    ins.then_inc(tt_zero, 1)
            pool.wait_ge(y_mm, NB5)
            for h in range(HEADS):
                pool.wait_ge(kin_done, h + 1)
                pool.wait_ge(dec_done, h + 1)
                if h:
                    pool.wait_ge(kt_mm, h)
                n = (NCK - 1) * CK
                plink(pool.tensor_tensor(kout[:, 0:n].rearrange("p (c t) -> p c t", t=CK),
                                         KH[:, h, 0:n].rearrange("p (c t) -> p c t", t=CK),
                                         dec[:, h, 0:NCK - 1].unsqueeze(2).to_broadcast([P, NCK - 1, CK]), ALU.mult))
                pairs = dec[:, h, 0:NCK - 1].rearrange("p (c r) -> p c r", r=2)
                first = kout[:, 0:n].rearrange("p (c r t) -> p c r t", r=2, t=CK)[:, :, 0, :]
                pool.tensor_tensor(first, first, pairs[:, :, 1].unsqueeze(2).to_broadcast([P, NB32, CK]), ALU.mult)\
                    .then_inc(kout_done, 1)
                pool.wait_ge(gsc_mm, h + 1)
                q2 = second(QH[:, h, 0:n])
                pool.tensor_tensor(q2, q2, pairs[:, :, 0].unsqueeze(2).to_broadcast([P, NB32, CK]), ALU.mult)\
                    .then_inc(q32_done, 1)


def kernel(**inputs):
    import concourse.bacc as bacc
    from concourse.bass_utils import run_bass_kernel_spmd

    nc = bacc.Bacc("TRN2", target_bir_lowering=False, num_devices=1)
    arrays, A = {}, {}
    for name in INPUTS + ["consts"]:
        a = host_constants() if name == "consts" else np.ascontiguousarray(inputs[name])
        arrays[f"in_{name}_dram"] = a
        A[name] = nc.dram_tensor(f"in_{name}_dram", a.shape, mybir.dt.from_np(a.dtype), kind="ExternalInput").ap()
    out = nc.dram_tensor("out_dram", (1, SEQ, D), F32, kind="ExternalOutput").ap()
    emit(nc, A, out)
    return run_bass_kernel_spmd(nc, [arrays], core_ids=[0]).results[0]["out_dram"]
```
